# Optimizing a Trainium2 kernel written in Bass

```python
import math
import jax, jax.numpy as jnp
from jax import lax
import numpy as np

D_MODEL = 1024
BATCH = 1
SEQ = 512
DEPTH = 2
DEC_BATCH = 8
DEC_SEQ = 16
PAST_LEN = 512

CHUNK = 64
N_MIXERS = 2
N_A_LAYERS = (DEPTH + 1) // 2
N_B_LAYERS = DEPTH // 2

A_HEADS = 16
A_HEAD_DIM = D_MODEL // A_HEADS
A_WIDTH = A_HEADS * A_HEAD_DIM
A_PAST_CHUNKS = 8
A_PAST = A_PAST_CHUNKS * CHUNK
A_BAND = A_PAST + CHUNK
REL_CLIP = 128

B_HEADS = 16
B_KV_HEADS = 4
B_HEAD_DIM = D_MODEL // B_HEADS
B_GROUP = B_HEADS // B_KV_HEADS
IDX_HEADS = 8
IDX_DIM = 64
TOPK_MAX = 256
B_QBLOCK = 64
B_Q = B_HEADS * B_HEAD_DIM
B_KV = B_KV_HEADS * B_HEAD_DIM
B_QI = IDX_HEADS * IDX_DIM
B_SPLITS = [B_Q, B_Q + B_KV, B_Q + 2 * B_KV, B_Q + 2 * B_KV + B_QI, B_Q + 2 * B_KV + B_QI + IDX_DIM]
B_IN = B_Q + 2 * B_KV + B_QI + IDX_DIM + IDX_HEADS

D_FF = 2816
ALPHA = (2.0 * DEPTH) ** 0.25
BETA = (8.0 * DEPTH) ** -0.25
LN_EPS = 1e-5

kernel_name = 'hybrid_streaming_encoder_step'

def layer_norm(x, g, b):
    xf = x.astype(jnp.float32)
    mu = jnp.mean(xf, axis=-1, keepdims=True)
    var = jnp.mean(jnp.square(xf - mu), axis=-1, keepdims=True)
    y = (xf - mu) * lax.rsqrt(var + LN_EPS) * g.astype(jnp.float32) + b.astype(jnp.float32)
    return y.astype(x.dtype)

def swiglu(x, wg, wu, wd):
    return (jax.nn.silu(x @ wg) * (x @ wu)) @ wd

def alibi_slopes(n):
    return 2.0 ** (-8.0 * jnp.arange(1, n + 1, dtype=jnp.float32) / n)

def _split_a(h):
    bsz, t, _ = h.shape
    q, k, v = jnp.split(h, 3, axis=-1)
    shp = (bsz, t, A_HEADS, A_HEAD_DIM)
    return q.reshape(shp), k.reshape(shp), v.reshape(shp)

def band_attention(q, k, v, q_pos, k_pos, k_valid, rel_bias):
    rel = jnp.clip(q_pos[:, None] - k_pos[None, :], -REL_CLIP, REL_CLIP) + REL_CLIP
    bias = rel_bias[:, rel].astype(jnp.float32)
    s = jnp.einsum('bqhd,bkhd->bhqk', q, k).astype(jnp.float32) * (A_HEAD_DIM ** -0.5) + bias
    s = jnp.where(k_valid[None, None, None, :], s, -jnp.inf)
    p = jax.nn.softmax(s, axis=-1).astype(v.dtype)
    return jnp.einsum('bhqk,bkhd->bqhd', p, v)

def mixer_a_prompt(x, w_in, rel_bias, w_out):
    bsz, s_len, _ = x.shape
    q, k, v = _split_a(x @ w_in)
    pad = ((0, 0), (A_PAST, 0), (0, 0), (0, 0))
    kp = jnp.pad(k, pad)
    vp = jnp.pad(v, pad)

    def one_chunk(c):
        start = c * CHUNK
        qc = lax.dynamic_slice_in_dim(q, start, CHUNK, axis=1)
        kc = lax.dynamic_slice_in_dim(kp, start, A_BAND, axis=1)
        vc = lax.dynamic_slice_in_dim(vp, start, A_BAND, axis=1)
        q_pos = start + jnp.arange(CHUNK)
        k_pos = start - A_PAST + jnp.arange(A_BAND)
        return band_attention(qc, kc, vc, q_pos, k_pos, k_pos >= 0, rel_bias)

    o = lax.map(one_chunk, jnp.arange(s_len // CHUNK))
    o = jnp.moveaxis(o, 0, 1).reshape(bsz, s_len, A_WIDTH)
    keep = min(A_PAST, s_len)
    return o @ w_out, k[:, s_len - keep:], v[:, s_len - keep:]

def mixer_a_sample(x, cache_k, cache_v, w_in, rel_bias, w_out):
    bsz, t, _ = x.shape
    n_cache = cache_k.shape[1]
    q, k, v = _split_a(x @ w_in)
    kk = jnp.concatenate([cache_k.astype(k.dtype), k], axis=1)
    vv = jnp.concatenate([cache_v.astype(v.dtype), v], axis=1)
    q_pos = PAST_LEN + jnp.arange(t)
    k_pos = PAST_LEN + jnp.arange(-n_cache, t)
    o = band_attention(q, kk, vv, q_pos, k_pos, k_pos >= 0, rel_bias)
    return o.reshape(bsz, t, A_WIDTH) @ w_out, k, v

def _split_b(h):
    bsz, t, _ = h.shape
    q, k, v, qi, ki, wi = jnp.split(h, B_SPLITS, axis=-1)
    return (q.reshape(bsz, t, B_HEADS, B_HEAD_DIM),
            k.reshape(bsz, t, B_KV_HEADS, B_HEAD_DIM),
            v.reshape(bsz, t, B_KV_HEADS, B_HEAD_DIM),
            qi.reshape(bsz, t, IDX_HEADS, IDX_DIM), ki, wi)

def sparse_attention(q, qi, wi, k, v, ki, q_pos, n_sel):
    bsz, nq = q.shape[:2]
    n_keys = k.shape[1]
    limit = (q_pos // CHUNK + 1) * CHUNK
    admissible = jnp.arange(n_keys)[None, :] < limit[:, None]
    dots = jnp.einsum('bqhd,bld->bqhl', qi.astype(jnp.float32), ki.astype(jnp.float32)) * (IDX_DIM ** -0.5)
    score = jnp.einsum('bqhl,bqh->bql', jax.nn.relu(dots), wi.astype(jnp.float32) * (IDX_HEADS ** -0.5))
    score = jnp.where(admissible[None], score, -jnp.inf)
    _, sel = lax.top_k(score, n_sel)
    sel_valid = sel < limit[None, :, None]
    k_sel = jax.vmap(lambda a, i: a[i])(k, sel)
    v_sel = jax.vmap(lambda a, i: a[i])(v, sel)
    qg = q.reshape(bsz, nq, B_KV_HEADS, B_GROUP, B_HEAD_DIM)
    s = jnp.einsum('bqkgd,bqnkd->bqkgn', qg, k_sel).astype(jnp.float32) * (B_HEAD_DIM ** -0.5)
    dist = jnp.abs(q_pos[None, :, None] - sel).astype(jnp.float32)
    slopes = alibi_slopes(B_HEADS).reshape(B_KV_HEADS, B_GROUP)
    s = s - slopes[None, None, :, :, None] * dist[:, :, None, None, :]
    s = jnp.where(sel_valid[:, :, None, None, :], s, -jnp.inf)
    p = jax.nn.softmax(s, axis=-1).astype(v.dtype)
    o = jnp.einsum('bqkgn,bqnkd->bqkgd', p, v_sel)
    return o.reshape(bsz, nq, B_Q)

def mixer_b_prompt(x, w_in, w_out):
    bsz, s_len, _ = x.shape
    q, k, v, qi, ki, wi = _split_b(x @ w_in)
    n_sel = min(TOPK_MAX, s_len // 4)

    def one_block(i):
        start = i * B_QBLOCK
        sl = lambda a: lax.dynamic_slice_in_dim(a, start, B_QBLOCK, axis=1)
        return sparse_attention(sl(q), sl(qi), sl(wi), k, v, ki, start + jnp.arange(B_QBLOCK), n_sel)

    o = lax.map(one_block, jnp.arange(s_len // B_QBLOCK))
    o = jnp.moveaxis(o, 0, 1).reshape(bsz, s_len, B_Q)
    return o @ w_out, k, v, ki

def mixer_b_sample(x, cache_k, cache_v, cache_idx, w_in, w_out):
    bsz, t, _ = x.shape
    past = cache_k.shape[1]
    q, k, v, qi, ki, wi = _split_b(x @ w_in)
    kk = jnp.concatenate([cache_k.astype(k.dtype), k], axis=1)
    vv = jnp.concatenate([cache_v.astype(v.dtype), v], axis=1)
    kki = jnp.concatenate([cache_idx.astype(ki.dtype), ki], axis=1)
    n_sel = min(TOPK_MAX, (past + t) // 4)
    o = sparse_attention(q, qi, wi, kk, vv, kki, past + jnp.arange(t), n_sel)
    return o @ w_out, k, v, ki

def half_ffn_block(x, wg, wu, wd, g, b):
    return layer_norm(ALPHA * x + 0.5 * swiglu(x, wg, wu, wd), g, b)

def setup_inputs(seed: int = 0) -> dict:
    key = jax.random.key(seed)
    ks = jax.random.split(key, 20)
    f32 = jnp.float32
    n_a_cache = min(A_PAST, PAST_LEN)

    def nrm(k, shape, scale):
        return jax.random.normal(k, shape, f32) * scale

    a_w_in = nrm(ks[8], (N_A_LAYERS, D_MODEL, 3 * A_WIDTH), D_MODEL ** -0.5)
    a_w_in = a_w_in.at[..., 2 * A_WIDTH:].multiply(BETA)
    b_w_in = nrm(ks[11], (N_B_LAYERS, D_MODEL, B_IN), D_MODEL ** -0.5)
    b_w_in = b_w_in.at[..., B_Q + B_KV:B_Q + 2 * B_KV].multiply(BETA)
    return {
        'x_prompt': nrm(ks[0], (BATCH, SEQ, D_MODEL), 1.0),
        'x_sample': nrm(ks[1], (DEC_BATCH, DEC_SEQ, D_MODEL), 1.0),
        'cache_a_k': nrm(ks[2], (N_A_LAYERS, DEC_BATCH, n_a_cache, A_HEADS, A_HEAD_DIM), 1.0),
        'cache_a_v': nrm(ks[3], (N_A_LAYERS, DEC_BATCH, n_a_cache, A_HEADS, A_HEAD_DIM), BETA),
        'cache_b_k': nrm(ks[4], (N_B_LAYERS, DEC_BATCH, PAST_LEN, B_KV_HEADS, B_HEAD_DIM), 1.0),
        'cache_b_v': nrm(ks[5], (N_B_LAYERS, DEC_BATCH, PAST_LEN, B_KV_HEADS, B_HEAD_DIM), BETA),
        'cache_b_idx': nrm(ks[6], (N_B_LAYERS, DEC_BATCH, PAST_LEN, IDX_DIM), 1.0),
        'ln_g': 1.0 + nrm(ks[7], (DEPTH, 3, D_MODEL), 0.02),
        'ln_b': nrm(ks[13], (DEPTH, 3, D_MODEL), 0.02),
        'ffn_w_gate': nrm(ks[14], (DEPTH, 2, D_MODEL, D_FF), D_MODEL ** -0.5),
        'ffn_w_up': nrm(ks[15], (DEPTH, 2, D_MODEL, D_FF), D_MODEL ** -0.5),
        'ffn_w_down': nrm(ks[16], (DEPTH, 2, D_FF, D_MODEL), BETA * D_FF ** -0.5),
        'a_w_in': a_w_in,
        'a_rel_bias': nrm(ks[9], (N_A_LAYERS, A_HEADS, 2 * REL_CLIP + 1), 0.5),
        'a_w_out': nrm(ks[10], (N_A_LAYERS, A_WIDTH, D_MODEL), BETA * A_WIDTH ** -0.5),
        'b_w_in': b_w_in,
        'b_w_out': nrm(ks[12], (N_B_LAYERS, B_Q, D_MODEL), BETA * B_Q ** -0.5),
    }

def reference(x_prompt, x_sample, cache_a_k, cache_a_v, cache_b_k, cache_b_v, cache_b_idx,
              ln_g, ln_b, ffn_w_gate, ffn_w_up, ffn_w_down,
              a_w_in, a_rel_bias, a_w_out, b_w_in, b_w_out):
    xp, xs = x_prompt, x_sample
    a_kp, a_vp, a_ks, a_vs = [], [], [], []
    b_kp, b_vp, b_ip, b_ks, b_vs, b_is = [], [], [], [], [], []
    for layer in range(DEPTH):
        mixer = layer % N_MIXERS
        j = layer // N_MIXERS
        ffn1 = (ffn_w_gate[layer, 0], ffn_w_up[layer, 0], ffn_w_down[layer, 0], ln_g[layer, 0], ln_b[layer, 0])
        xp = half_ffn_block(xp, *ffn1)
        xs = half_ffn_block(xs, *ffn1)
        if mixer == 0:
            yp, kp, vp = mixer_a_prompt(xp, a_w_in[j], a_rel_bias[j], a_w_out[j])
            ys, k_s, v_s = mixer_a_sample(xs, cache_a_k[j], cache_a_v[j], a_w_in[j], a_rel_bias[j], a_w_out[j])
            a_kp.append(kp); a_vp.append(vp); a_ks.append(k_s); a_vs.append(v_s)
        else:
            yp, kp, vp, ip = mixer_b_prompt(xp, b_w_in[j], b_w_out[j])
            ys, k_s, v_s, i_s = mixer_b_sample(xs, cache_b_k[j], cache_b_v[j], cache_b_idx[j], b_w_in[j], b_w_out[j])
            b_kp.append(kp); b_vp.append(vp); b_ip.append(ip)
            b_ks.append(k_s); b_vs.append(v_s); b_is.append(i_s)
        xp = layer_norm(ALPHA * xp + yp, ln_g[layer, 1], ln_b[layer, 1])
        xs = layer_norm(ALPHA * xs + ys, ln_g[layer, 1], ln_b[layer, 1])
        ffn2 = (ffn_w_gate[layer, 1], ffn_w_up[layer, 1], ffn_w_down[layer, 1], ln_g[layer, 2], ln_b[layer, 2])
        xp = half_ffn_block(xp, *ffn2)
        xs = half_ffn_block(xs, *ffn2)
    a_k_prompt = jnp.stack(a_kp, 0)
    a_v_prompt = jnp.stack(a_vp, 0)
    a_k_sample = jnp.stack(a_ks, 0)
    a_v_sample = jnp.stack(a_vs, 0)
    b_k_prompt = jnp.stack(b_kp, 0)
    b_v_prompt = jnp.stack(b_vp, 0)
    b_idx_prompt = jnp.stack(b_ip, 0)
    b_k_sample = jnp.stack(b_ks, 0)
    b_v_sample = jnp.stack(b_vs, 0)
    b_idx_sample = jnp.stack(b_is, 0)
    return (xp, xs, a_k_prompt, a_v_prompt, a_k_sample, a_v_sample,
            b_k_prompt, b_v_prompt, b_idx_prompt, b_k_sample, b_v_sample, b_idx_sample)


_drawn_inputs = setup_inputs


def setup_inputs(seed=0):
    import zlib

    import numpy as np

    out = dict(_drawn_inputs(seed))
    spreads = {}
    factors = {'cache_a_k': 3.735, 'cache_a_v': 2.944, 'a_rel_bias': 4.789}
    for name, (base, spread) in spreads.items():
        noise = np.random.default_rng([zlib.crc32(name.encode()), seed]).standard_normal(out[name].shape)
        drawn = base * np.exp(spread * noise) if base else spread * noise
        out[name] = __import__('jax').numpy.asarray(drawn.astype(out[name].dtype))
    for name, factor in factors.items():
        out[name] = (out[name] * factor).astype(out[name].dtype)
    return out
```

```python
from contextlib import ExitStack

import concourse.bass as bass
from concourse import mybir
from concourse.alu_op_type import AluOpType as ALU

ACT = mybir.ActivationFunctionType
F32 = mybir.dt.float32
F32R = mybir.dt.float32r
ds = bass.ds
P = 128
BIG = 1e30
TAKEN = -3e38


def row(t, i):
    if isinstance(i, int):
        return t[:, i, :]
    return t[:, ds(i, 1), :].rearrange("p a n -> p (a n)")


def hybrid_encoder_step(nc, io):
    SEQ, D = io["x_prompt"].shape[1:]
    NB, NT = io["x_sample"].shape[:2]
    F = io["ffn_w_gate"].shape[3]
    PAST = io["cache_a_k"].shape[2]
    H, DH = io["cache_a_k"].shape[3:]
    KV = io["cache_b_k"].shape[3]
    IH = io["b_w_in"].shape[2] - D - 2 * KV * DH
    IH = (IH - DH) // (DH + 1)
    CLIP = (io["a_rel_bias"].shape[2] - 1) // 2
    KD = D // P
    QT = SEQ // P
    TT = QT + NB * NT // P
    T = TT * P
    TH = T // 2
    FH = F // P // 2
    KMAX = max(FH, KD)
    NK = PAST + NT
    KT_ = PAST // P
    CH = 64
    LAG = 3
    ALPHA = 4.0 ** 0.25
    EPS = 1e-5
    SEL_P = min(256, SEQ // 4)
    SEL_S = min(256, NK // 4)
    L_EXT = NK + P

    UP, DOWN = FH, KD // 2
    FFN = 2 * (UP + DOWN)
    A_Q, A_K, A_V = 4, 4, 4
    A_IN, A_OUT, B_OUT = A_Q + A_K + A_V, 4, 4
    B_IN = 9
    ffn_base = [0, FFN + A_IN + A_OUT, 2 * FFN + A_IN + A_OUT, 3 * FFN + A_IN + A_OUT + B_IN + B_OUT]
    a_in, a_out = FFN, FFN + A_IN
    b_in = ffn_base[2] + FFN
    b_out = b_in + B_IN
    NORM_OF = [0, 2, 3, 5]
    UNITS_P = 4 * H
    UNITS_S = 2 * NB
    UNITS = UNITS_P + UNITS_S

    with ExitStack() as ctx:
        def sb(name, shape, dt=F32, c=ctx):
            return c.enter_context(nc.sbuf_tensor(name, shape, dt))

        def sem(name):
            return ctx.enter_context(nc.semaphore(name))

        def sems(name):
            return [sem(f"{name}{s}") for s in range(2)]

        xres = sb("xres", [P, KD, T])
        raw = [sb(f"raw{s}", [P, KMAX, P]) for s in range(2)]
        wh = [sb(f"wh{s}", [P, KMAX, P], F32R) for s in range(2)]
        wl = [sb(f"wl{s}", [P, KMAX, P], F32R) for s in range(2)]
        ident = sb("ident", [P, P])
        ones = sb("ones", [P, 1])
        one = sb("one", [P, P])
        eps = sb("eps", [P, 1])
        g_t = sb("g_t", [P, 6 * KD])
        b_t = sb("b_t", [P, 6 * KD])
        nat = sb("nat", [P, 2, T])
        big = sb("big", [P, 8, T])
        mx = sb("mx", [P, 2])
        rsum = sb("rsum", [P, 2])
        rinv = sb("rinv", [P, 2])
        zsum, qsum, sil, hf = (big[:, i, :] for i in (0, 1, 4, 5))
        diag = big[:, 2:4, :]
        sq = big[:, 6:8, :]
        stage = [sil, hf]
        score = [big[:, 0, :], big[:, 1, :]]
        prob = [big[:, 2, :], big[:, 3, :]]
        prob_t = sq
        v_new = [hf, sil]

        same_t = sb("same_t", [P, P])
        rep = sb("rep", [8, P])
        nslope = sb("nslope", [P, H])
        nslope_s = sb("nslope_s", [P, 2])
        nsl8 = sb("nsl8", [8, 2])
        frame = sb("frame", [P, 1])
        top8 = sb("top8", [P, 4, 8])
        mean, mean2, var, std, rstd = (sb(n, [P, TT]) for n in ("mean", "mean2", "var", "std", "rstd"))

        R0 = 88064

        def layout(name, first, second):
            with ExitStack() as c:
                got = [sb(n, s, d, c) for n, s, d in first]
                used = 0
                for n, s, d in first:
                    size = 4
                    for x in s[1:]:
                        size *= x
                    used += size
                assert used <= R0, (name, used)
                sb(f"{name}_pad", [P, (R0 - used) // 4], F32, c)
                return got + [sb(n, s, d, c) for n, s, d in second]

        hh, hl, xh, xl = layout("ffn", [("hh", [P, FH, T], F32R), ("hl", [P, FH, T], F32R)],
                                [("xh", [P, KD, T], F32R), ("xl", [P, KD, T], F32R)])
        xnat, lnraw = layout("pro", [("xnat", [P, TT, D], F32), ("lnraw", [6 * KD, 2, P], F32)], [])
        (a_qT, a_kT, a_v, a_kc_t, a_toep, a_bias_s, a_qb, a_kc, a_vc, a_qz) = layout(
            "a", [("a_qT", [P, KD, T], F32), ("a_kT", [P, KD, T], F32), ("a_v", [P, TT, D], F32),
                  ("a_kc_t", [P, 2, 4, NK], F32), ("a_toep", [P, 2, SEQ], F32),
                  ("a_bias_s", [P, 2, NK], F32), ("a_qb", [P, 2, P], F32)],
            [("a_kc", [P, 2, KT_, D // 2], F32), ("a_vc", [P, 2, KT_, D // 2], F32), ("a_qz", [P, 4, SEQ], F32)])
        a_onat = layout("ao", [("a_skip", [P, 2 * KD * T + TT * D], F32), ("a_onat", [P, QT, D], F32)], [])[1]
        (b_qT, b_kT, b_v, qiT, kiT, w_nat, dist, seen, b_mask_s, work, ki_c, ki_ct, lw, qib,
         b_kc_t, b_onat, b_qb, b_kc, b_vc, b_qz) = layout(
            "b", [("b_qT", [P, KD, T], F32), ("b_kT", [P, 2, T], F32), ("b_v", [P, TT, KV * DH], F32),
                  ("qiT", [P, 4, T], F32), ("kiT", [P, T], F32), ("w_nat", [P, TT, IH], F32),
                  ("dist", [P, SEQ], F32), ("seen", [P, 1280], F32), ("b_mask_s", [P, 2, NK], F32),
                  ("work", [P, 1152 + NK], F32), ("ki_c", [P, 2, KT_, DH], F32), ("ki_ct", [DH, 2, PAST], F32),
                  ("lw", [P, 9 * P], F32), ("qib", [DH, 2, P], F32)],
            [("b_kc_t", [P, 2, 1, NK], F32), ("b_onat", [P, QT, D], F32), ("b_qb", [P, 2, P], F32),
             ("b_kc", [P, 2, KT_, P], F32), ("b_vc", [P, 2, KT_, P], F32), ("b_qz", [P, 4, SEQ], F32)])
        ps = ctx.enter_context(nc.psum_tensor("ps", [P, 8, 512], F32))
        flat = ps[:, :, :].rearrange("p b n -> p (b n)")
        skewed = nc.dram_tensor("skewed", (H, P, L_EXT + P), F32, kind="Internal").ap()
        seen_tab = nc.dram_tensor("seen_tab", (P, NK), F32, kind="Internal").ap()

        raw_loaded = sems("raw_loaded")
        w_hi = sems("w_hi")
        w_lo = sems("w_lo")
        mm_done = sems("mm_done")
        out_taken = sems("out_taken")
        h_hi = sem("h_hi")
        h_lo = sem("h_lo")
        s_in = sem("s_in")
        s_const = sem("s_const")
        zsum_done = sem("zsum_done")
        sq_done = sem("sq_done")
        qsum_done = sem("qsum_done")
        mean_done = sem("mean_done")
        msq_done = sem("msq_done")
        mean_copied = sem("mean_copied")
        m2_done = sem("m2_done")
        var_done = sem("var_done")
        std_done = sem("std_done")
        rstd_done = sem("rstd_done")
        diag_done = sem("diag_done")
        spread = sem("spread")
        centred = sem("centred")
        scaled = sem("scaled")
        x_ready = sem("x_ready")
        xh_ready = sem("xh_ready")
        xl_ready = sem("xl_ready")
        s_ln = sem("s_ln")
        y_turned = sem("y_turned")
        y_copied = sem("y_copied")
        x_turned = sem("x_turned")
        nat_stored = sems("nat_stored")
        v_stored = sem("v_stored")
        nat_turned = sems("nat_turned")
        nat_taken = sems("nat_taken")
        kt_copied = sem("kt_copied")
        s_done = sem("s_done")
        score_begun = sem("score_begun")
        score_done = sem("score_done")
        exp_done = sem("exp_done")
        rinv_done = sem("rinv_done")
        prob_turned = sem("prob_turned")
        prob_t_ready = sem("prob_t_ready")
        o_done = sem("o_done")
        o_taken = sem("o_taken")
        pnorm_done = sem("pnorm_done")
        qz_zero = sem("qz_zero")
        qz_ready = sem("qz_ready")
        toep_loaded = sems("toep_loaded")
        bias_ready = sem("bias_ready")
        onat_turned = sem("onat_turned")
        onat_taken = sems("onat_taken")
        k_loaded = sems("k_loaded")
        v_loaded = sems("v_loaded")
        kx_done = sems("kx_done")
        kx_taken = sems("kx_taken")
        qb_ready = sem("qb_ready")
        qb_zero = sem("qb_zero")
        oh_ready = sem("oh_ready")
        ol_ready = sem("ol_ready")
        tab_in = sem("tab_in")
        tab_built = sem("tab_built")
        tab_stored = sem("tab_stored")
        bias_s_loaded = sem("bias_s_loaded")
        ki_loaded = sems("ki_loaded")
        ix_mm = sem("ix_mm")
        ix_relu = sem("ix_relu")
        ix_acc = sem("ix_acc")
        ki_turned = sem("ki_turned")
        ki_ready = sem("ki_ready")
        qib_ready = sem("qib_ready")
        lw_ready = sem("lw_ready")
        lw_mm = sem("lw_mm")
        ws_mm = sem("ws_mm")
        top_done = sem("top_done")
        cut_done = sem("cut_done")
        seen_done = sem("seen_done")
        seen_stored = sem("seen_stored")
        mask_loaded = sems("mask_loaded")
        const_b = sem("const_b")
        dist_done = sem("dist_done")
        slope_mm = sem("slope_mm")

        def out2(s):
            return ps[:, 2 * s:2 * s + 2, 0:TH]

        spread_ps = [flat[:, 2048:2048 + T], flat[:, 3072:3072 + T]]

        def two(ap):
            return ap.rearrange("p (c n) -> p c n", c=2)

        MIX = [dict(qT=a_qT, kT=a_kT, v=a_v, onat=a_onat, kc=a_kc, vc=a_vc, kc_t=a_kc_t, qb=a_qb, qz=a_qz,
                    pairs=4, kin=io["cache_a_k"], vin=io["cache_a_v"]),
               dict(qT=b_qT, kT=b_kT, v=b_v, onat=b_onat, kc=b_kc, vc=b_vc, kc_t=b_kc_t, qb=b_qb, qz=b_qz,
                    pairs=1, kin=io["cache_b_k"], vin=io["cache_b_v"])]

        def key_place(m, j):
            return (j // 2, j % 2) if m == 0 else (0, j // 4)

        def qz_slot(m, j):
            part = key_place(m, j)[1]
            return 2 * part + (j // 2 if m == 0 else j) % 2

        def kx_index(m, b, s, p):
            if m == 0:
                return b * 4 + (2 * s + p // 2)
            return b + 4 * NB

        def kx_bank(m, s, p):
            return p % 2 if m == 0 else s

        def pipelined(e, lags, body):
            def step(t, s, b_of, live):
                for k, lag in enumerate(lags):
                    if live(lag):
                        body(b_of((s - lag) // 2), (s - lag) % 2, k)
            first = (max(lags) + 1) // 2 * 2
            for t in range(first):
                step(t, t % 2, lambda d: t // 2 + d, lambda lag: t >= lag)
            with e.Fori(first // 2, NB) as b:
                for s in range(2):
                    step(None, s, lambda d: b + d, lambda lag: True)
            for t in range(2 * NB, 2 * NB + max(lags)):
                step(t, t % 2, lambda d: t // 2 + d, lambda lag: t - lag < 2 * NB)

        block = ctx.enter_context(nc.Block())

        @block.sync
        def _(sp):
            sp.dma_start(xnat[:, 0:TT - 1, :], io["x_prompt"].rearrange("o (j p) d -> p (o j) d", p=P)).then_inc(s_in, 16)
            sp.dma_start(xnat[:, TT - 1, :], io["x_sample"].rearrange("b t d -> (b t) d")).then_inc(s_in, 16)
            sp.dma_start(lnraw[:, 0, :], io["ln_g"].rearrange("l j (k p) -> (l j k) p", p=P)).then_inc(s_in, 16)
            sp.dma_start(lnraw[:, 1, :], io["ln_b"].rearrange("l j (k p) -> (l j k) p", p=P)).then_inc(s_in, 16)
            sp.dma_start(nat[0:H, 0, 0:2 * CLIP + 1], io["a_rel_bias"][0]).then_inc(tab_in, 16)

            def load(s, n, src):
                sp.wait_ge(w_lo[s], n + 1)
                cols = src.shape[2]
                sp.dma_start(raw[s][:, 0:src.shape[1], 0:cols], src).then_inc(raw_loaded[s], 16)

            def load_tiles(w, n, i):
                for s in range(2):
                    load(s, n, w[:, :, ds(i * (2 * P) + s * P, P)])

            def ffn(f, skip):
                wg, wu, wd = (io[w][f // 2, f % 2].rearrange("(k p) c -> p k c", p=P)
                              for w in ("ffn_w_gate", "ffn_w_up", "ffn_w_down"))
                for half in range(2):
                    base = ffn_base[f] + half * (UP + DOWN)
                    with sp.Fori(skip if half == 0 else 0, UP) as i:
                        load(0, i + base, wg[:, :, ds((i + half * FH) * P, P)])
                        load(1, i + base, wu[:, :, ds((i + half * FH) * P, P)])
                    with sp.Fori(0, DOWN) as i:
                        for s in range(2):
                            load(s, i + (base + UP), wd[:, half * FH:(half + 1) * FH, ds(i * (2 * P) + s * P, P)])

            def store_tile(s, cols, dst_p, dst_s):
                view = nat[:, s, :].rearrange("p (j c) -> p j c", c=P)[:, :, 0:cols]
                sp.dma_start(dst_p, view[:, 0:QT, :]).then_inc(nat_stored[s], 16)
                sp.dma_start(dst_s, view[:, QT, :]).then_inc(nat_stored[s], 16)

            def rows_of(name, prompt):
                ap = io[name][0]
                if len(ap.shape) == 4:
                    ap = ap.rearrange("a b h d -> a b (h d)")
                return ap.rearrange("o (j p) c -> p (o j) c", p=P) if prompt else ap.rearrange("b t c -> (b t) c")

            def store_v(m):
                sp.wait_ge(nat_taken[0], 9 if m == 0 else 12)
                sp.wait_ge(nat_taken[1], 9 if m == 0 else 12)
                mix = MIX[m]
                sp.dma_start(rows_of("ab"[m] + "_v_prompt", True), mix["v"][:, 0:QT, :]).then_inc(v_stored, 16)
                sp.dma_start(rows_of("ab"[m] + "_v_sample", False), mix["v"][:, QT, :]).then_inc(v_stored, 16)

            def cached(m):
                mix = MIX[m]
                w = mix["pairs"] * P
                kin = mix["kin"][0].rearrange("b (j p) h d -> b p j (h d)", p=P)
                vin = mix["vin"][0].rearrange("b (j p) h d -> b p j (h d)", p=P)

                def unit(b, s, k):
                    waits = not isinstance(b, int) or b > 0
                    if k == 0:
                        if waits:
                            for bank in {kx_bank(m, s, p) for p in range(mix["pairs"])}:
                                p, ago = (2 + bank, 4) if m == 0 else (0, 1)
                                sp.wait_ge(kx_done[bank], kx_index(m, b, s, p) + (1 - ago))
                        kc = kin[ds(b, 1), :, :, s * w:(s + 1) * w].rearrange("o p j c -> p (o j) c")
                        sp.dma_start(mix["kc"][:, s, :, :], kc).then_inc(k_loaded[s], 16)
                        if m == 1:
                            if waits:
                                sp.wait_ge(bias_ready, b * 2 + (H + UNITS_P + s - 1))
                            sp.dma_start(b_mask_s[:, s, :], seen_rows(b)).then_inc(mask_loaded[s], 16)
                    else:
                        if waits:
                            sp.wait_ge(o_done, b * 2 + (m * UNITS + UNITS_P + s + 1))
                        vc = vin[ds(b, 1), :, :, s * w:(s + 1) * w].rearrange("o p j c -> p (o j) c")
                        sp.dma_start(mix["vc"][:, s, :, :], vc).then_inc(v_loaded[s], 16)
                        src = io["ab"[m] + "_v_sample"][0][ds(b, 1)].rearrange("o t h d -> (o t) (h d)")
                        sp.dma_start(v_new[s][0:NT, 0:w], src[:, s * w:(s + 1) * w]).then_inc(v_loaded[s], 16)

                def seen_rows(b):
                    return bass.AP(tensor=seen_tab.tensor, offset=b * (NT * NK), ap=[[0, 8], [NK, NT], [1, NK]])

                pipelined(sp, (0, 3), unit)

            sp.wait_ge(tab_built, 2)
            tab = big[0:H, 6:8, :].rearrange("p a n -> p (a n)")[:, 0:L_EXT]
            sp.dma_start(bass.AP(tensor=skewed.tensor, offset=0, ap=[[P * (L_EXT + P), H], [L_EXT + P + 1, P], [1, L_EXT]]),
                         tab.unsqueeze(1).to_broadcast([H, P, L_EXT])).then_inc(tab_stored, 16)
            ffn(0, 0)
            wa = io["a_w_in"][0].rearrange("(k p) c -> p k c", p=P)
            with sp.Fori(0, A_Q + 2) as i:
                load_tiles(wa, i + a_in, i)
            with sp.Fori(0, A_K) as i:
                load_tiles(wa, i + (a_in + A_Q + 2), i + (A_Q + 2))
                for s in range(2):
                    sp.wait_ge(nat_taken[s], i + 2)
                    c = ds(i * (2 * P) + s * P, P)
                    store_tile(s, P, rows_of("a_k_prompt", True)[:, :, c], rows_of("a_k_sample", False)[:, c])
            with sp.Fori(0, 2) as i:
                load_tiles(wa, i + (a_in + A_Q + A_K + 2), i + (A_Q + A_K + 2))
            wo = io["a_w_out"][0].rearrange("(k p) c -> p k c", p=P)
            with sp.Fori(0, 2) as i:
                load_tiles(wo, i + a_out, i)
            sp.wait_ge(tab_stored, 16)
            for s in range(2):
                sp.wait_ge(mm_done[s], a_out + 1)
            for s in range(2):
                sp.dma_start(a_bias_s[:, s, :], skewed[8 * s:8 * s + 8, 0:NT, NK - PAST:2 * NK - PAST]).then_inc(bias_s_loaded, 16)
            store_v(0)
            for h in range(H):
                if h >= 2:
                    sp.wait_ge(score_done, 4 * (h - 1) + 2)
                sp.dma_start(a_toep[:, h % 2, :], skewed[h, :, NK - (SEQ - P):NK + P]).then_inc(toep_loaded[h % 2], 16)
            sp.wait_ge(v_stored, 32)
            cached(0)
            with sp.Fori(2, 4) as i:
                load_tiles(wo, i + a_out, i)
            ffn(1, 0)
            ffn(2, 0)
            wb = io["b_w_in"][0].rearrange("(k p) c -> p k c", p=P)
            q0, k0, v0, i0 = 0, D, D + KV * DH, D + 2 * KV * DH
            ki0 = i0 + IH * DH
            load_tiles(wb[:, :, i0:ki0], b_in, 0)
            load_tiles(wb[:, :, i0:ki0], b_in + 1, 1)
            load(0, b_in + 2, wb[:, :, ki0:ki0 + DH])
            load(1, b_in + 2, wb[:, :, ki0 + DH:ki0 + DH + IH])
            load_tiles(wb, b_in + 3, 0)
            load_tiles(wb, b_in + 4, 1)
            for s in range(2):
                sp.wait_ge(mm_done[s], b_in + 1)
            for b in range(NB):
                if b >= 2:
                    sp.wait_ge(ki_turned, b - 1)
                sp.dma_start(ki_c[:, b % 2, :, :], io["cache_b_idx"][0, b].rearrange("(j p) d -> p j d", p=P)).then_inc(ki_loaded[b % 2], 16)
            sp.wait_ge(nat_taken[0], 2 + A_K + A_V)
            store_tile(0, DH, rows_of("b_idx_prompt", True), rows_of("b_idx_sample", False))
            load_tiles(wb, b_in + 5, 2)
            load_tiles(wb, b_in + 6, 3)
            for s in range(2):
                load(s, b_in + 7, wb[:, :, k0 + s * P:k0 + (s + 1) * P])
            for s in range(2):
                load(s, b_in + 8, wb[:, :, v0 + s * P:v0 + (s + 1) * P])
            wo = io["b_w_out"][0].rearrange("(k p) c -> p k c", p=P)
            load_tiles(wo, b_out, 0)
            for s in range(2):
                sp.wait_ge(nat_taken[s], 3 + A_K + A_V)
                store_tile(s, P, rows_of("b_k_prompt", True)[:, :, s * P:(s + 1) * P],
                           rows_of("b_k_sample", False)[:, s * P:(s + 1) * P])
            load_tiles(wo, b_out + 1, 1)
            store_v(1)
            sp.wait_ge(seen_done, 9)
            sp.dma_start(seen_tab, work[:, 1152:1152 + NK]).then_inc(seen_stored, 16)
            sp.wait_ge(v_stored, 64)
            sp.wait_ge(seen_stored, 16)
            cached(1)
            with sp.Fori(2, 4) as i:
                load_tiles(wo, i + b_out, i)
            ffn(3, 0)
            for k in range(KD):
                sp.wait_ge(y_copied, k + 1)
                c = slice(P * k, P * (k + 1))
                store_tile(k % 2, P, io["y_prompt"][0, :, c].rearrange("(j p) c -> p j c", p=P),
                           io["y_sample"][:, :, c].rearrange("b t c -> (b t) c"))
            for s in range(2):
                sp.wait_ge(nat_stored[s], 32 * ([6, 5][s] + KD // 2))

        @block.gpsimd
        def _(pool):
            for s in range(2):
                pool.sem_inc(w_lo[s], 1)
            for s in (pnorm_done, pnorm_done):
                pool.sem_inc(s, 1)
            nc.gpsimd.memset(ident[:], 0.0).then_inc(s_const, 1)
            nc.gpsimd.memset(ones[:], 1.0 / D).then_inc(s_const, 1)
            nc.gpsimd.memset(eps[:], EPS).then_inc(s_const, 1)
            nc.gpsimd.memset(one[:], 1.0).then_inc(s_const, 1)
            pool.wait_ge(s_const, 4)
            nc.gpsimd.affine_select(out=ident[:], in_=ident[:], compare_op=ALU.not_equal, fill=1.0, base=0,
                                    pattern=[[-1, P]], channel_multiplier=1).then_inc(s_const, 1)

            def split_low(s, n, kt):
                pool.wait_ge(w_hi[s], n + 1)
                nc.gpsimd.tensor_tensor(wl[s][:, 0:kt, :], raw[s][:, 0:kt, :], wh[s][:, 0:kt, :].bitcast(F32),
                                        ALU.subtract).then_inc(w_lo[s], 1)

            def steps(base, count, kt, kt_next):
                if count > 1:
                    with pool.Fori(0, count - 1) as i:
                        for s in range(2):
                            split_low(s, i + (base + 1), kt)
                if kt_next:
                    for s in range(2):
                        split_low(s, base + count, kt_next)

            def x_low(base):
                for k in range(KD):
                    pool.wait_ge(xh_ready, base + k + 1)
                    pool.wait_ge(x_ready, base + k + 1)
                    nc.gpsimd.tensor_tensor(xl[:, k, :], xres[:, k, :], xh[:, k, :].bitcast(F32),
                                            ALU.subtract).then_inc(xl_ready, 1)

            def ffn(f, kt_next):
                for half in range(2):
                    base = ffn_base[f] + half * (UP + DOWN)
                    steps(base, UP, KD, FH)
                    steps(base + UP, DOWN, FH, kt_next if half else KD)

            def constants_b():
                nc.gpsimd.memset(same_t[:], 0.0).then_inc(const_b, 1)
                for d in range(-7, 8):
                    pool.wait_ge(const_b, d + 8)
                    nc.gpsimd.affine_select(out=same_t[:], in_=same_t[:], compare_op=ALU.not_equal, fill=1.0,
                                            base=NT * d, pattern=[[-1, P]], channel_multiplier=1).then_inc(const_b, 1)
                nc.gpsimd.memset(rep[:], 1.0).then_inc(const_b, 1)
                pool.wait_ge(const_b, 17)
                nc.gpsimd.affine_select(out=rep[:], in_=rep[:], compare_op=ALU.is_ge, fill=0.0,
                                        base=0, pattern=[[1, P]], channel_multiplier=-NT).then_inc(const_b, 1)
                pool.wait_ge(const_b, 18)
                nc.gpsimd.affine_select(out=rep[:], in_=rep[:], compare_op=ALU.is_ge, fill=0.0,
                                        base=NT - 1, pattern=[[-1, P]], channel_multiplier=NT).then_inc(const_b, 1)
                for h in range(H):
                    nc.gpsimd.memset(nslope[:, h:h + 1], -(2.0 ** (-8.0 * (h + 1) / H))).then_inc(const_b, 1)

            def zero_buffers(m):
                mix = MIX[m]
                last = a_out if m == 0 else b_out
                for s in range(2):
                    pool.wait_ge(mm_done[s], last + 1)
                nc.gpsimd.memset(mix["qz"][:], 0.0).then_inc(qz_zero, 1)
                nc.gpsimd.memset(mix["qb"][:], 0.0).then_inc(qb_zero, 1)

            def normalise(m):
                for u in range(UNITS_S):
                    cg = m * UNITS + UNITS_P + u
                    if m == 1:
                        mask_bias(u, cg)
                    pool.wait_ge(rinv_done, cg + 3)
                    pr = prob[u % 2][:, 0:NK]
                    nc.gpsimd.tensor_scalar(pr, pr, rinv[:, u % 2:u % 2 + 1], 1.0, ALU.mult, ALU.mult).then_inc(pnorm_done, 1)

            def mask_bias(u, cg):
                pool.wait_ge(mask_loaded[u % 2], 16 * (u // 2 + 1))
                pool.wait_ge(score_done, cg + 1)
                nc.gpsimd.tensor_scalar(nat[:, u % 2, 0:NK], b_mask_s[:, u % 2, :], nslope_s[:, u % 2:u % 2 + 1], 1.0,
                                        ALU.mult, ALU.mult).then_inc(bias_ready, 1)

            for s in range(2):
                split_low(s, 0, KD)
            x_low(0)
            constants_b()
            ffn(0, KD)
            x_low(KD)
            steps(a_in, A_IN, KD, KD)
            zero_buffers(0)
            for h in range(H):
                pool.wait_ge(toep_loaded[h % 2], 16 * (h // 2 + 1))
                nc.gpsimd.memset(a_toep[0:CH, h % 2, SEQ - CH:SEQ], -BIG).then_inc(bias_ready, 1)
            normalise(0)
            steps(a_out, A_OUT, KD, KD)
            x_low(2 * KD)
            ffn(1, KD)
            x_low(3 * KD)
            ffn(2, KD)
            x_low(4 * KD)
            pool.wait_ge(mm_done[0], b_in + 1)
            pool.wait_ge(mm_done[1], b_in + 1)
            nc.gpsimd.iota(dist[:], pattern=[[-1, SEQ]], base=SEQ - P, channel_multiplier=1,
                           allow_small_or_imprecise_dtypes=True).then_inc(dist_done, 1)
            nc.gpsimd.memset(lw[:], 0.0).then_inc(dist_done, 1)
            nc.gpsimd.iota(b_mask_s[:, 0, :], pattern=[[-1, NK]], base=PAST, channel_multiplier=0,
                           allow_small_or_imprecise_dtypes=True).then_inc(dist_done, 1)
            nc.gpsimd.iota(b_mask_s[:, 1, 0:NT], pattern=[[1, NT]], base=0, channel_multiplier=0,
                           allow_small_or_imprecise_dtypes=True).then_inc(dist_done, 1)
            steps(b_in, B_IN, KD, KD)
            zero_buffers(1)
            pool.wait_ge(seen_done, 9)
            pool.wait_ge(nat_stored[0], 32 * 6)
            pool.wait_ge(nat_stored[1], 32 * 5)
            for h in range(H):
                for qt in range(QT):
                    c = UNITS + 4 * h + qt
                    pool.wait_ge(score_done, c + 1)
                    off = [0, 128, 384, 768][qt]
                    nc.gpsimd.tensor_scalar(nat[:, c % 2, 0:P * (qt + 1)], seen[:, off:off + P * (qt + 1)],
                                            nslope[:, h:h + 1], 1.0, ALU.mult, ALU.mult).then_inc(bias_ready, 1)
            normalise(1)
            steps(b_out, B_OUT, KD, KD)
            x_low(5 * KD)
            ffn(3, None)

        @block.scalar
        def _(act):
            def split_high(s, n, kt):
                act.wait_ge(raw_loaded[s], n * 16 + 16)
                act.wait_ge(mm_done[s], n + 1)
                nc.scalar.activation(wh[s][:, 0:kt, :], raw[s][:, 0:kt, :], ACT.Copy).then_inc(w_hi[s], 1)

            def up_step(n, i, kt_next):
                split_high(0, n + 1, kt_next)
                act.wait_ge(mm_done[0], n + 2)
                act.wait_ge(out_taken[1], n + 1)
                nc.scalar.activation(two(sil), out2(0), ACT.Silu).then_inc(out_taken[0], 1)
                split_high(1, n + 1, kt_next)
                act.wait_ge(out_taken[1], n + 2)
                nc.scalar.activation(row(hh, i), hf, ACT.Copy).then_inc(h_hi, 1)

            def down_step(n, i, kt_next, norm, final=False):
                for s in range(2):
                    if kt_next and not (final and s):
                        split_high(s, n + 1, kt_next)
                    if norm is not None:
                        act.wait_ge(out_taken[s], n + 2)
                        act.wait_ge(qsum_done, i * 2 + (norm * (KD + 1) + 1))
                        nc.scalar.activation(sq[:, s, :], row(xres, i * 2 + s), ACT.Square).then_inc(sq_done, 1)
                if kt_next and final:
                    split_high(1, n + 1, kt_next)

            def down(base, norm, kt, kt_next):
                with act.Fori(0, DOWN - 1) as i:
                    down_step(i + base, i, kt, norm)
                down_step(base + DOWN - 1, DOWN - 1, kt_next, norm, final=True)

            def norm(L, last=False):
                act.wait_ge(var_done, L + 1)
                nc.scalar.activation(std[:], var[:], ACT.Sqrt, bias=eps[:, 0:1]).then_inc(std_done, 1)
                for k in range(KD):
                    act.wait_ge(scaled, L * KD + k + 1)
                    g, b = (t[:, L * KD + k:L * KD + k + 1] for t in (g_t, b_t))
                    if not last:
                        nc.scalar.activation(xh[:, k, :], sq[:, k % 2, :], ACT.Identity, scale=g, bias=b).then_inc(xh_ready, 1)
                    nc.scalar.activation(xres[:, k, :], sq[:, k % 2, :], ACT.Identity, scale=g, bias=b).then_inc(x_ready, 1)

            def ffn(f, kt_next):
                for half in range(2):
                    base = ffn_base[f] + half * (UP + DOWN)
                    with act.Fori(0, UP - 1) as i:
                        up_step(i + base, i, KD)
                    up_step(base + UP - 1, UP - 1, FH)
                    down(base + UP, NORM_OF[f] if half else None, FH, kt_next if half else KD)

            def project(n, dst, scale=1.0):
                for s in range(2):
                    act.wait_ge(mm_done[s], n + 2)
                    nc.scalar.activation(two(dst(s)), out2(s), ACT.Copy, scale=scale).then_inc(out_taken[s], 1)
                    split_high(s, n + 1, KD)

            def to_stage(n, t, scales=(1.0, 1.0)):
                for s in range(2):
                    act.wait_ge(mm_done[s], n + 2)
                    act.wait_ge(nat_taken[s], t + 1)
                    nc.scalar.activation(two(stage[s]), out2(s), ACT.Copy, scale=scales[s]).then_inc(out_taken[s], 1)
                    split_high(s, n + 1, KD)

            def exps(cg, s, w):
                act.wait_ge(score_done, cg + 3)
                act.wait_ge(prob_turned, cg + 1)
                act.wait_ge(rinv_done, cg + 1)
                nc.scalar.activation(prob[s][:, 0:w], score[s][:, 0:w], ACT.Exp, bias=mx[:, s:s + 1], scale=-1.0,
                                     accum_out=rsum[:, s:s + 1]).then_inc(exp_done, 1)

            def take_turned(cg, s, w):
                act.wait_ge(prob_turned, cg + 3)
                act.wait_ge(o_done, cg + 1)
                nc.scalar.activation(prob_t[:, s, 0:w], ps[:, 2 + s, 0:w], ACT.Copy).then_inc(prob_t_ready, 1)

            def attention(m):
                with act.Fori(0, 2) as g:
                    for c in range(32 + 1):
                        if c < 32:
                            exps(g * 32 + (m * UNITS + c), c % 2, P * (c % QT + 1))
                        if c >= 1:
                            take_turned(g * 32 + (m * UNITS + c - 1), (c - 1) % 2, P * ((c - 1) % QT + 1))
                for k in range(0, KD, 2):
                    act.wait_ge(onat_turned, m * KD + k + 1)
                    nc.scalar.activation(MIX[m]["qT"][:, k, 0:SEQ], ps[:, 6, :], ACT.Copy).then_inc(onat_taken[0], 1)
                mix = MIX[m]

                def stage(b, s, k):
                    cg = b * 2 + (m * UNITS + UNITS_P + s)
                    if k == 0:
                        for p in range(mix["pairs"]):
                            if kx_bank(m, s, p) == 0:
                                i = kx_index(m, b, s, p)
                                act.wait_ge(kx_done[0], i + 1)
                                act.wait_ge(s_done, cg - 1)
                                nc.scalar.activation(mix["kc_t"][:, s, p, 0:PAST], ps[:, 6, :], ACT.Copy).then_inc(kx_taken[0], 1)
                    elif k == 1:
                        exps(cg, s, NK)
                    else:
                        act.wait_ge(prob_turned, cg + 3)
                        act.wait_ge(o_done, cg + 1)
                        nc.scalar.activation(prob_t[:, s, 0:PAST], ps[:, 2 + s, :], ACT.Copy)
                        nc.scalar.activation(prob_t[0:NT, s, PAST:PAST + P], ps[0:NT, 4 + s, 256:256 + P], ACT.Copy).then_inc(prob_t_ready, 1)
                pipelined(act, (0, 1, 2), stage)

            for s in range(2):
                act.sem_inc(mm_done[s], 1)
                act.sem_inc(out_taken[s], 1)
                for t in (exp_done, prob_t_ready, prob_turned, o_done):
                    act.sem_inc(t, 1)
            for s in range(2):
                split_high(s, 0, KD)
            for k in range(KD):
                act.wait_ge(x_turned, k + 1)
                nc.scalar.activation(xres[:, k, :], flat[:, 1024 * (k % 2):1024 * (k % 2) + T], ACT.Copy).then_inc(x_ready, 1)
            ffn(0, KD)
            norm(0)
            with act.Fori(0, A_Q) as i:
                project(i + a_in, lambda s: row(a_qT, i * 2 + s), DH ** -0.5)
            with act.Fori(0, A_K + A_V) as i:
                to_stage(i + (a_in + A_Q), i)
            attention(0)
            down(a_out, 1, KD, KD)
            norm(1)
            ffn(1, KD)
            norm(2)
            ffn(2, KD)
            norm(3)
            NAT_B = A_K + A_V
            with act.Fori(0, 2) as i:
                project(i + b_in, lambda s: row(qiT, i * 2 + s), DH ** -0.5)
            to_stage(b_in + 2, NAT_B, (1.0, IH ** -0.5))
            for i in range(3 * IH + NB):
                act.wait_ge(ix_mm, i + 1)
                if i >= 2:
                    if i < 3 * IH + 2:
                        act.wait_ge(ix_acc, min(i - 1, 3 * IH))
                    if i >= 3 * IH + 2:
                        act.wait_ge(ws_mm, i - 3 * IH - 1)
                if i < 3 * IH:
                    w = P * (i // IH + 2)
                    nc.scalar.activation(score[i % 2][:, 0:w], ps[:, 4 + i % 2, 0:w], ACT.Relu).then_inc(ix_relu, 1)
                else:
                    nc.scalar.activation(score[i % 2][:, 0:NK], flat[:, 2048:2048 + NK], ACT.Relu).then_inc(ix_relu, 1)
            with act.Fori(0, 4) as i:
                project(i + (b_in + 3), lambda s: row(b_qT, i * 2 + s), DH ** -0.5)
            to_stage(b_in + 7, NAT_B + 1)
            to_stage(b_in + 8, NAT_B + 2)
            attention(1)
            down(b_out, 4, KD, KD)
            norm(4)
            ffn(3, None)
            norm(5, last=True)

        @block.vector
        def _(dve):
            def x_high(k, base):
                dve.wait_ge(x_ready, base + k + 1)
                nc.vector.tensor_copy(xh[:, k, :], xres[:, k, :]).then_inc(xh_ready, 1)

            def up_step(n, i, hs):
                dve.wait_ge(mm_done[1], n + 2)
                dve.wait_ge(out_taken[0], n + 2)
                dve.wait_ge(h_lo, hs + 1)
                nc.vector.scalar_tensor_tensor(out=two(hf), in0=two(sil), scalar=0.5, in1=out2(1),
                                               op0=ALU.mult, op1=ALU.mult).then_inc(out_taken[1], 1)
                dve.wait_ge(h_hi, hs + 1)
                nc.vector.tensor_tensor(row(hl, i), hf, row(hh, i).bitcast(F32), ALU.subtract).then_inc(h_lo, 1)

            def down_step(n, i, first, norm, final=False):
                for s in range(2):
                    z = row(xres, i * 2 + s)
                    dve.wait_ge(mm_done[s], n + 2)
                    nc.vector.scalar_tensor_tensor(out=two(z), in0=two(z), scalar=ALPHA if first else 1.0,
                                                   in1=out2(s), op0=ALU.mult, op1=ALU.add).then_inc(out_taken[s], 1)
                    if norm is not None:
                        if not (final and s == 1):
                            dve.wait_ge(out_taken[s], n + 2)
                            dve.wait_ge(zsum_done, i * 2 + (norm * KD + s + 1))
                            nc.vector.tensor_tensor(zsum, zsum, z, ALU.add).then_inc(zsum_done, 1)
                        dve.wait_ge(sq_done, i * 2 + (norm * KD + s + 1))
                        dve.wait_ge(qsum_done, i * 2 + (norm * (KD + 1) + s + 1))
                        nc.vector.tensor_tensor(qsum, qsum, sq[:, s, :], ALU.add).then_inc(qsum_done, 1)

            def down(base, first, norm):
                if norm is not None:
                    nc.vector.memset(zsum, 0.0).then_inc(zsum_done, 1)
                    nc.vector.memset(qsum, 0.0).then_inc(qsum_done, 1)
                with dve.Fori(0, DOWN - 1) as i:
                    down_step(i + base, i, first, norm)
                down_step(base + DOWN - 1, DOWN - 1, first, norm, final=True)

            def on_diagonals(i, stat):
                nc.vector.tensor_tensor(diag[:, i, :].rearrange("p (j n) -> p j n", n=P),
                                        ident[:].unsqueeze(1).to_broadcast([P, TT, P]),
                                        stat[:].unsqueeze(2).to_broadcast([P, TT, P]), ALU.mult).then_inc(diag_done, 1)

            def norm(L):
                dve.wait_ge(mean_done, L + 1)
                nc.vector.tensor_copy(mean[:], ps[:, 6, 0:TT]).then_inc(mean_copied, 1)
                dve.wait_ge(mean_copied, L + 1)
                nc.vector.tensor_tensor(mean2[:], mean[:], mean[:], ALU.mult).then_inc(m2_done, 1)
                on_diagonals(0, mean)
                dve.wait_ge(m2_done, L + 1)
                dve.wait_ge(msq_done, L + 1)
                nc.vector.tensor_tensor(var[:], ps[:, 7, 0:TT], mean2[:], ALU.subtract).then_inc(var_done, 1)
                dve.wait_ge(std_done, L + 1)
                nc.vector.reciprocal(rstd[:], std[:]).then_inc(rstd_done, 1)
                dve.wait_ge(rstd_done, L + 1)
                on_diagonals(1, rstd)
                dve.wait_ge(spread, 2 * L + 1)
                for k in range(KD + 1):
                    if k < KD:
                        nc.vector.tensor_tensor(xres[:, k, :], xres[:, k, :], spread_ps[0], ALU.subtract).then_inc(centred, 1)
                    if k >= 1:
                        dve.wait_ge(centred, L * KD + k)
                        if k == 1:
                            dve.wait_ge(spread, 2 * L + 2)
                        if k >= 3:
                            dve.wait_ge(x_ready, (L + 1) * KD + k - 2)
                        nc.vector.tensor_tensor(sq[:, (k - 1) % 2, :], xres[:, k - 1, :], spread_ps[1],
                                                ALU.mult).then_inc(scaled, 1)

            def ffn(f):
                for half in range(2):
                    base = ffn_base[f] + half * (UP + DOWN)
                    with dve.Fori(0, UP) as i:
                        up_step(i + base, i, i + (2 * f + half) * UP)
                    if f == 0 and half:
                        dve.wait_ge(tab_stored, 16)
                    down(base + UP, half == 0, NORM_OF[f] if half else None)

            def turned(s):
                return flat[:, 2048 + 1024 * s:2048 + 1024 * s + T].rearrange("p (j c) -> p j c", c=P)

            def keys(m, n, i, t, stores):
                for s in range(2):
                    dve.wait_ge(out_taken[s], n + 2)
                    nc.vector.tensor_copy(row(MIX[m]["kT"], i * 2 + s), stage[s]).then_inc(kt_copied, 1)
                    dve.wait_ge(nat_turned[s], t + 1)
                    if stores[s] is not None:
                        dve.wait_ge(nat_stored[s], stores[s])
                    nc.vector.tensor_copy(nat[:, s, :].rearrange("p (j c) -> p j c", c=P), turned(s)).then_inc(nat_taken[s], 1)

            def values(m, n, i, t):
                for s in range(2):
                    dve.wait_ge(nat_turned[s], t + 1)
                    nc.vector.tensor_copy(MIX[m]["v"][:, :, ds(i * (2 * P) + s * P, P)], turned(s)).then_inc(nat_taken[s], 1)

            def copy_q(m, g, j):
                mix = MIX[m]
                part = key_place(m, j)[1]
                src = row(mix["qT"], g * 4 + j // 2)[DH * (j % 2):DH * (j % 2 + 1), 0:SEQ]
                nc.vector.tensor_copy(mix["qz"][DH * part:DH * (part + 1), qz_slot(m, j), :], src).then_inc(qz_ready, 1)

            def bias_scores(cg, s, w, scores, bias):
                dve.wait_ge(s_done, cg + 1)
                dve.wait_ge(exp_done, cg + 1)
                dve.sem_inc(score_begun, 1)
                nc.vector.tensor_tensor_reduce(out=score[s][:, 0:w], in0=scores, in1=bias, scale=-1.0, scalar=3e38,
                                               op0=ALU.add, op1=ALU.min, accum_out=mx[:, s:s + 1]).then_inc(score_done, 1)

            def invert_sum(cg, s):
                dve.wait_ge(exp_done, cg + 3)
                dve.wait_ge(o_taken, cg + 1)
                nc.vector.reciprocal(rinv[:, s:s + 1], rsum[:, s:s + 1]).then_inc(rinv_done, 1)

            def attention(m):
                mix = MIX[m]
                dve.wait_ge(qz_zero, m + 1)
                with dve.Fori(0, 2) as g:
                    for c in range(32 + 2):
                        if c < 32:
                            j, qt, w = c // 4, c % 4, P * (c % 4 + 1)
                            cg = g * 32 + (m * UNITS + c)
                            if c == 0:
                                copy_q(m, g, 0)
                            if qt == 0 and j + 1 < 8:
                                copy_q(m, g, j + 1)
                            if m == 0:
                                if qt == 0:
                                    dve.wait_ge(bias_ready, g * 8 + (j + 1))
                                bias = a_toep[:, j % 2, SEQ - w:SEQ]
                            else:
                                dve.wait_ge(bias_ready, g * 32 + (H + c + 1))
                                bias = nat[:, c % 2, 0:w]
                            bias_scores(cg, c % 2, w, ps[:, c % 2, 0:w], bias)
                        if 1 <= c < 33:
                            invert_sum(g * 32 + (m * UNITS + c - 1), (c - 1) % 2)
                        if c >= 2:
                            x = c - 2
                            dve.wait_ge(o_done, g * 32 + (m * UNITS + x + 3))
                            dve.wait_ge(rinv_done, g * 32 + (m * UNITS + x + 3))
                            nc.vector.tensor_scalar(mix["onat"][:, x % 4, ds(g * (8 * DH) + x // 4 * DH, DH)],
                                                    ps[:, 4 + x % 2, 0:DH], rinv[:, x % 2:x % 2 + 1], None,
                                                    ALU.mult).then_inc(o_taken, 1)
                for k in range(1, KD, 2):
                    dve.wait_ge(onat_turned, m * KD + k + 1)
                    nc.vector.tensor_copy(mix["qT"][:, k, 0:SEQ], ps[:, 7, :]).then_inc(onat_taken[1], 1)
                if m == 0:
                    dve.wait_ge(bias_s_loaded, 16 * 2)
                dve.wait_ge(qb_zero, m + 1)
                dve.wait_ge(o_taken, m * UNITS + UNITS_P + 2)

                def frames(b):
                    return ds(b * NT + SEQ, NT)

                def unit(b, s, k):
                    cg = b * 2 + (m * UNITS + UNITS_P + s)
                    qT, qb, t = mix["qT"], mix["qb"], frames(b)
                    if k == 0:
                        dve.wait_ge(s_done, cg - 1)
                        if m == 0:
                            v = qb[:, s, :].rearrange("p (a x) -> p a x", x=2 * NT)
                            nc.vector.tensor_copy(mix["kc_t"][:, s, :, PAST:NK], mix["kT"][:, 4 * s:4 * s + 4, t])
                            nc.vector.tensor_copy(v[0:DH, :, 0:NT], qT[0:DH, 4 * s:4 * s + 4, t])
                            nc.vector.tensor_copy(v[DH:P, :, NT:2 * NT], qT[DH:P, 4 * s:4 * s + 4, t]).then_inc(qb_ready, 1)
                        else:
                            v = qb[:, s, :].rearrange("p (a e n) -> p a e n", e=2, n=NT)
                            nc.vector.tensor_copy(mix["kc_t"][:, s, :, PAST:NK], mix["kT"][:, s:s + 1, t])
                            for kv in range(2):
                                for e in range(2):
                                    q = nc.vector.tensor_copy(v[DH * kv:DH * (kv + 1), 2 * kv:2 * kv + 2, e, :],
                                                              qT[DH * e:DH * (e + 1), 4 * s + 2 * kv:4 * s + 2 * kv + 2, t])
                            q.then_inc(qb_ready, 1)
                        for p in range(mix["pairs"]):
                            if kx_bank(m, s, p) == 1:
                                dve.wait_ge(kx_done[1], kx_index(m, b, s, p) + 1)
                                nc.vector.tensor_copy(mix["kc_t"][:, s, p, 0:PAST], ps[:, 7, :]).then_inc(kx_taken[1], 1)
                    elif k == 1:
                        if m == 1:
                            dve.wait_ge(bias_ready, b * 2 + (H + UNITS_P + s + 1))
                        bias_scores(cg, s, NK, flat[:, 0:NK], a_bias_s[:, s, :] if m == 0 else nat[:, s, 0:NK])
                        dve.wait_ge(pnorm_done, b * 2 + (m * UNITS_S + s + 1))
                        dve.wait_ge(exp_done, cg + 3)
                        nc.vector.reciprocal(rinv[:, s:s + 1], rsum[:, s:s + 1]).then_inc(rinv_done, 1)
                    else:
                        dve.wait_ge(o_done, cg + 3)
                        o = ps[:, 4 + s, 0:P]
                        if m == 0:
                            v = o.rearrange("p (a x) -> p a x", x=2 * NT)
                            nc.vector.tensor_copy(qT[0:DH, 4 * s:4 * s + 4, t], v[0:DH, :, 0:NT])
                            q = nc.vector.tensor_copy(qT[DH:P, 4 * s:4 * s + 4, t], v[DH:P, :, NT:2 * NT])
                        else:
                            v = o.rearrange("p (a e n) -> p a e n", e=2, n=NT)
                            for kv in range(2):
                                for e in range(2):
                                    q = nc.vector.tensor_copy(qT[DH * e:DH * (e + 1), 4 * s + 2 * kv:4 * s + 2 * kv + 2, t],
                                                              v[DH * kv:DH * (kv + 1), 2 * kv:2 * kv + 2, e, :])
                        q.then_inc(o_taken, 1)
                pipelined(dve, (0, 1, 3), unit)
                dve.wait_ge(o_taken, (m + 1) * UNITS + 2)
                dve.wait_ge(onat_taken[0], (m + 1) * KD // 2)
                for k in range(KD):
                    nc.vector.tensor_copy(xh[:, k, :], mix["qT"][:, k, :]).then_inc(oh_ready, 1)
                    dve.wait_ge(oh_ready, m * KD + k + 1)
                    nc.vector.tensor_tensor(xl[:, k, :], mix["qT"][:, k, :], xh[:, k, :].bitcast(F32),
                                            ALU.subtract).then_inc(ol_ready, 1)

            def selection():
                dve.wait_ge(dist_done, 4)
                nc.vector.scalar_tensor_tensor(out=dist[:], in0=dist[:], scalar=-1.0, in1=dist[:], op0=ALU.mult,
                                               op1=ALU.max).then_inc(cut_done, 1)
                nc.vector.tensor_tensor_reduce(out=qib_scratch, in0=same_t[:, 0:NT], in1=b_mask_s[:, 1, 0:NT], scale=1.0,
                                               scalar=0.0, op0=ALU.mult, op1=ALU.add, accum_out=frame[:]).then_inc(cut_done, 1)
                dve.wait_ge(cut_done, 2)
                nc.vector.memset(dist[0:CH, SEQ - CH:SEQ], BIG).then_inc(cut_done, 1)
                nc.vector.tensor_scalar(b_mask_s[:, 0, :], b_mask_s[:, 0, :], frame[:, 0:1], None, ALU.add).then_inc(cut_done, 1)
                dve.wait_ge(cut_done, 4)
                nc.vector.scalar_tensor_tensor(out=b_mask_s[:, 0, :], in0=b_mask_s[:, 0, :], scalar=-1.0,
                                               in1=b_mask_s[:, 0, :], op0=ALU.mult, op1=ALU.max).then_inc(cut_done, 1)
                t = A_K + A_V
                dve.wait_ge(out_taken[0], b_in + 4)
                nc.vector.tensor_copy(kiT[0:DH, :], stage[0][0:DH, :])
                nc.vector.tensor_copy(kiT[DH:P, :], stage[0][0:DH, :]).then_inc(kt_copied, 1)
                dve.wait_ge(nat_turned[0], t + 1)
                dve.wait_ge(nat_stored[0], 32 * 4)
                nc.vector.tensor_copy(nat[:, 0, :].rearrange("p (j c) -> p j c", c=P)[:, :, 0:DH],
                                      turned(0)[:, :, 0:DH]).then_inc(nat_taken[0], 1)
                dve.wait_ge(nat_turned[1], t + 1)
                nc.vector.tensor_copy(w_nat[:], turned(1)[:, :, 0:IH]).then_inc(nat_taken[1], 1)
                dve.wait_ge(lw_mm, 1)
                nc.vector.tensor_tensor(lw[:].rearrange("p (b x) -> p b x", x=P + NT)[:, :, 0:NT],
                                        ps[:, 2, 0:P].rearrange("p (b x) -> p b x", x=NT),
                                        same_t[:].rearrange("p (b x) -> p b x", x=NT), ALU.mult).then_inc(lw_ready, 1)
                def stream(b):
                    v = qib[:, b % 2, :].rearrange("p (a e n) -> p a e n", e=2, n=NT)
                    f = slice(SEQ + NT * b, SEQ + NT * (b + 1))
                    if b >= 2:
                        dve.wait_ge(ix_mm, 3 * IH + b - 1)
                    nc.vector.tensor_copy(v[:, :, 0, :], qiT[0:DH, :, f])
                    nc.vector.tensor_copy(v[:, :, 1, :], qiT[DH:P, :, f]).then_inc(qib_ready, 1)
                    dve.wait_ge(ki_turned, b + 1)
                    nc.vector.tensor_copy(ki_ct[:, b % 2, :], ps[0:DH, b % 2, :]).then_inc(ki_ready, 1)

                dve.wait_ge(nat_taken[1], t + 2)
                for i in range(3 * IH):
                    q, h = i // IH + 1, i % IH
                    w, off = P * (q + 1), [0, 0, 256, 640][q]
                    dve.wait_ge(ix_relu, i + 1)
                    wk = work[:, off:off + w]
                    if h == 0:
                        nc.vector.tensor_scalar(wk, score[i % 2][:, 0:w], w_nat[:, q, 0:1], None, ALU.mult).then_inc(ix_acc, 1)
                    else:
                        dve.wait_ge(ix_acc, i)
                        nc.vector.scalar_tensor_tensor(out=wk, in0=score[i % 2][:, 0:w], scalar=w_nat[:, q, h:h + 1],
                                                       in1=wk, op0=ALU.mult, op1=ALU.add).then_inc(ix_acc, 1)
                dve.wait_ge(ix_acc, 3 * IH)
                tiles = []
                for q in range(1, QT):
                    w, off = P * (q + 1), [0, 0, 256, 640][q]
                    nc.vector.memset(work[0:CH, off + w - CH:off + w], TAKEN).then_inc(cut_done, 1)
                    tiles.append(work[:, off:off + w])
                for b in range(NB):
                    stream(b)
                dve.wait_ge(ws_mm, NB)
                tiles.append(work[:, 1152:1152 + NK])
                nc.vector.tensor_copy(tiles[3], flat[:, 3072:3072 + NK]).then_inc(cut_done, 1)
                n_cut, n_top = 5 + QT, 0
                rounds = [(SEL_P + 7) // 8] * 3 + [(SEL_S + 7) // 8]
                for r in range(max(rounds)):
                    live = [x for x in range(4) if r < rounds[x]]
                    first_cut, first_top = n_cut, n_top
                    for x in live:
                        dve.wait_ge(cut_done, max(first_cut - len(live), 0) + 1 + live.index(x) if r and len(live) == 4 else first_cut)
                        nc.vector.max(top8[:, x, :], tiles[x]).then_inc(top_done, 1)
                        n_top += 1
                    rest = SEL_S % 8 if r == rounds[3] - 1 else 0
                    if rest:
                        dve.wait_ge(top_done, n_top)
                        nc.vector.memset(top8[:, 3, rest:8], TAKEN).then_inc(top_done, 1)
                        n_top += 1
                    for y, x in enumerate(live):
                        dve.wait_ge(top_done, n_top if rest else first_top + y + 1)
                        nc.vector.match_replace(tiles[x], top8[:, x, :], tiles[x], TAKEN).then_inc(cut_done, 1)
                        n_cut += 1
                dve.wait_ge(cut_done, n_cut)
                nc.vector.tensor_copy(seen[:, 0:P], dist[:, SEQ - P:SEQ]).then_inc(seen_done, 1)
                outs = [seen[:, 128:384], seen[:, 384:768], seen[:, 768:1280], tiles[3]]
                for x in range(4):
                    nc.vector.tensor_scalar(outs[x], tiles[x], TAKEN / 2, BIG, ALU.is_gt, ALU.mult).then_inc(seen_done, 1)
                for x in range(4):
                    dve.wait_ge(seen_done, 2 + x)
                    d = b_mask_s[:, 0, :] if x == 3 else dist[:, SEQ - P * (x + 2):SEQ]
                    nc.vector.tensor_tensor(outs[x], outs[x], d, ALU.add).then_inc(seen_done, 1)

            qib_scratch = work[:, 0:NT]

            for s in range(2):
                for t in (score_done, rinv_done, o_taken):
                    dve.sem_inc(t, 1)
                dve.sem_inc(nat_taken[s], 1)
                dve.sem_inc(kx_taken[s], 1)
            dve.sem_inc(h_lo, 1)
            dve.wait_ge(tab_in, 16)
            tab = big[0:H, 6:8, :].rearrange("p a n -> p (a n)")
            rb = nat[0:H, 0, 0:2 * CLIP + 1]
            nc.vector.tensor_copy(tab[:, NK - CLIP:L_EXT], rb[:, 0:CLIP + P]).then_inc(tab_built, 1)
            nc.vector.tensor_copy(tab[:, 0:NK - CLIP], rb[:, 0:1].to_broadcast([H, NK - CLIP])).then_inc(tab_built, 1)
            dve.wait_ge(s_ln, 1)
            nc.vector.tensor_copy(g_t[:], ps[:, 4, 0:6 * KD]).then_inc(s_const, 1)
            nc.vector.tensor_copy(b_t[:], ps[:, 4, 64:64 + 6 * KD]).then_inc(s_const, 1)
            for k in range(KD):
                x_high(k, 0)
            dve.wait_ge(const_b, 19 + H)
            for s in range(2):
                if s:
                    dve.wait_ge(slope_mm, 1)
                nc.vector.tensor_tensor_reduce(out=top8[0:8, s, :], in0=ident[0:8, 0:8], in1=nslope[0:8, 8 * s:8 * s + 8],
                                               scale=1.0, scalar=0.0, op0=ALU.mult, op1=ALU.add,
                                               accum_out=nsl8[:, s:s + 1]).then_inc(slope_mm, 1)
            dve.wait_ge(slope_mm, 3)
            nc.vector.tensor_copy(nslope_s[:], ps[:, 5, 0:2]).then_inc(s_const, 1)
            ffn(0)
            norm(0)
            keys(0, a_in + A_Q, 0, 0, [None, None])
            with dve.Fori(1, A_K) as i:
                keys(0, i + (a_in + A_Q), i, i, [i * 32, i * 32])
            with dve.Fori(0, A_V) as i:
                values(0, i + (a_in + A_Q + A_K), i, i + A_K)
            attention(0)
            down(a_out, True, 1)
            norm(1)
            ffn(1)
            norm(2)
            ffn(2)
            norm(3)
            selection()
            keys(1, b_in + 7, 0, A_K + A_V + 1, [32 * 5, 32 * 4])
            values(1, b_in + 8, 0, A_K + A_V + 2)
            attention(1)
            down(b_out, True, 4)
            norm(4)
            ffn(3)
            norm(5)
            for k in range(KD):
                dve.wait_ge(y_turned, k + 1)
                dve.wait_ge(nat_stored[k % 2], 32 * ([6, 5][k % 2] + k // 2))
                nc.vector.tensor_copy(nat[:, k % 2, :], flat[:, 1024 * (k % 2):1024 * (k % 2) + T]).then_inc(y_copied, 1)

        @block.tensor
        def _(pe):
            def unit(s, n, kt, xa, xb, before=None):
                pe.wait_ge(w_lo[s], n + 2)
                pe.wait_ge(out_taken[s], n + 1)
                for k in range(kt):
                    if before:
                        before(k)
                    for j, (w, x) in enumerate(((wh[s], xa), (wh[s], xb), (wl[s], xa))):
                        for c in range(2):
                            mm = nc.tensor.matmul(ps[:, 2 * s + c, 0:TH], w[:, k, :], x[:, k, TH * c:TH * (c + 1)],
                                                  start=k == 0 and j == 0, stop=k == kt - 1 and j == 2)
                mm.then_inc(mm_done[s], 1)

            def first_pair(n, high, low, base):
                def products(s, parts, k, last=False):
                    for w, x in parts:
                        for c in range(2):
                            mm = nc.tensor.matmul(ps[:, 2 * s + c, 0:TH], w[:, k, :], x[:, k, TH * c:TH * (c + 1)],
                                                  start=k == 0 and w is wh[s] and x is xh, stop=last and x is xl)
                    if last:
                        mm.then_inc(mm_done[s], 1)

                for s in range(2):
                    pe.wait_ge(w_lo[s], n + 2)
                    pe.wait_ge(out_taken[s], n + 1)
                for t in range(KD + LAG):
                    if t < KD:
                        pe.wait_ge(high, base + t + 1)
                        products(0, [(wh[0], xh), (wl[0], xh)], t)
                    if 1 <= t <= KD:
                        pe.wait_ge(low, base + t)
                        products(0, [(wh[0], xl)], t - 1, t == KD)
                    if t >= LAG:
                        products(1, [(wh[1], xh), (wl[1], xh), (wh[1], xl)], t - LAG, t == KD + LAG - 1)

            def pairs(base, first, count, kt, xa, xb):
                if count > first:
                    with pe.Fori(first, count) as i:
                        for s in range(2):
                            unit(s, i + base, kt, xa, xb)

            def ffn(f, x_base):
                for half in range(2):
                    base = ffn_base[f] + half * (UP + DOWN)
                    hs = (2 * f + half) * UP
                    if half == 0:
                        first_pair(base, xh_ready, xl_ready, x_base)
                    pairs(base, 1 - half, UP, KD, xh, xl)

                    def wait_h(k):
                        if k in (0, FH - 1):
                            pe.wait_ge(h_lo, hs + (FH if k == 0 else FH + 1))
                    unit(0, base + UP, FH, hh, hl, wait_h)
                    unit(1, base + UP, FH, hh, hl)
                    pairs(base + UP, 1, DOWN, FH, hh, hl)

            def statistics(L, n):
                def sums(bank, of, first, last):
                    for j in range(TT):
                        mm = nc.tensor.matmul(ps[:, bank, j:j + 1], of[:, P * j:P * (j + 1)], ones[:, 0:1],
                                              start=first and j == 0, stop=last and j == TT - 1)
                    return mm
                pe.wait_ge(zsum_done, (L + 1) * KD)
                sums(6, zsum, True, False)
                pe.wait_ge(out_taken[1], n + 2)
                sums(6, xres[:, KD - 1, :], False, True).then_inc(mean_done, 1)
                pe.wait_ge(qsum_done, (L + 1) * (KD + 1))
                sums(7, qsum, True, True).then_inc(msq_done, 1)
                for i in range(2):
                    pe.wait_ge(diag_done, 2 * L + i + 1)
                    if i:
                        pe.wait_ge(var_done, L + 1)
                    for lo, hi in ((0, 512), (512, T)):
                        mm = nc.tensor.matmul(spread_ps[i][:, lo:hi], one[:], diag[:, i, lo:hi], start=True, stop=True)
                    mm.then_inc(spread, 1)

            def turn(n, t, rows=(P, P), before=None):
                for s in range(2):
                    pe.wait_ge(out_taken[s], n + 2)
                    pe.wait_ge(nat_taken[s], t + 1)
                    if before and s:
                        before()
                    r = rows[s]
                    for j in range(TT):
                        o = 2048 + 1024 * s + P * j
                        mm = nc.tensor.transpose(flat[:, o:o + r], stage[s][0:r, P * j:P * (j + 1)], ident[0:r, 0:r])
                    mm.then_inc(nat_turned[s], 1)

            def attention(m):
                mix = MIX[m]

                def scores(g, c):
                    j, qt, cg = c // 4, c % 4, g * 32 + (m * UNITS + c)
                    if qt == 0:
                        pe.wait_ge(qz_ready, g * 8 + (m * H + j + 1))
                    pe.wait_ge(score_done, cg + 1)
                    tile = g * 4 + j // 2 if m == 0 else g
                    nc.tensor.matmul(ps[:, c % 2, 0:P * (qt + 1)], mix["qz"][:, qz_slot(m, j), P * qt:P * (qt + 1)],
                                     row(mix["kT"], tile)[:, 0:P * (qt + 1)], start=True, stop=True).then_inc(s_done, 1)

                def turn_probs(g, c):
                    qt, cg = c % 4, g * 32 + (m * UNITS + c)
                    pe.wait_ge(exp_done, cg + 3)
                    pe.wait_ge(prob_t_ready, cg + 1)
                    for k in range(qt + 1):
                        mm = nc.tensor.transpose(ps[:, 2 + c % 2, P * k:P * (k + 1)], prob[c % 2][:, P * k:P * (k + 1)], ident[:])
                    mm.then_inc(prob_turned, 1)

                def outputs(g, c):
                    j, qt, cg = c // 4, c % 4, g * 32 + (m * UNITS + c)
                    pe.wait_ge(prob_t_ready, cg + 3)
                    pe.wait_ge(o_taken, cg + 1)
                    col = g * (8 * DH) + j * DH if m == 0 else g * (2 * DH) + j // 4 * DH
                    for k in range(qt + 1):
                        mm = nc.tensor.matmul(ps[:, 4 + c % 2, 0:DH], prob_t[:, c % 2, P * k:P * (k + 1)],
                                              mix["v"][:, k, ds(col, DH)], start=k == 0, stop=k == qt)
                    mm.then_inc(o_done, 1)

                with pe.Fori(0, 2) as g:
                    for c in range(32 + 2):
                        if c < 32:
                            scores(g, c)
                        if 1 <= c < 33:
                            turn_probs(g, c - 1)
                        if c >= 2:
                            outputs(g, c - 2)
                pe.wait_ge(o_taken, m * UNITS + UNITS_P + 2)
                for k in range(KD):
                    if k >= 2:
                        pe.wait_ge(onat_taken[k % 2], (m * KD + k) // 2)
                    for q in range(QT):
                        mm = nc.tensor.transpose(ps[:, 6 + k % 2, P * q:P * (q + 1)], mix["onat"][:, q, P * k:P * (k + 1)], ident[:])
                    mm.then_inc(onat_turned, 1)
                for s in range(2):
                    pe.wait_ge(onat_taken[s], (m + 1) * KD // 2)
                n_pairs = mix["pairs"]
                M = P // n_pairs

                def stream(b, s, k):
                    cg = b * 2 + (m * UNITS + UNITS_P + s)
                    if k == 0:
                        pe.wait_ge(k_loaded[s], b * 16 + 16 * (m * NB + 1))
                        for p in range(n_pairs):
                            bank = kx_bank(m, s, p)
                            pe.wait_ge(kx_taken[bank], kx_index(m, b, s, p) + 1)
                            for q in range(KT_):
                                mm = nc.tensor.transpose(ps[:, 6 + bank, P * q:P * (q + 1)],
                                                         mix["kc"][:, s, q, P * p:P * (p + 1)], ident[:])
                            mm.then_inc(kx_done[bank], 1)
                    elif k == 1:
                        for bank in {kx_bank(m, s, p) for p in range(n_pairs)}:
                            p = n_pairs - 2 + bank if m == 0 else 0
                            pe.wait_ge(kx_taken[bank], kx_index(m, b, s, p) + 2)
                        pe.wait_ge(qb_ready, b * 2 + (m * UNITS_S + s + 1))
                        pe.wait_ge(score_done, cg + 2)
                        for p in range(n_pairs):
                            for lo, hi in ((0, PAST), (PAST, NK)):
                                mm = nc.tensor.matmul(flat[M * p:M * (p + 1), lo:hi], mix["qb"][:, s, M * p:M * (p + 1)],
                                                      mix["kc_t"][:, s, p, lo:hi], start=True, stop=True)
                        mm.then_inc(s_done, 1)
                    elif k == 2:
                        pe.wait_ge(pnorm_done, b * 2 + (m * UNITS_S + s + 3))
                        pe.wait_ge(prob_t_ready, cg + 1)
                        pe.wait_ge(o_taken, cg + 1)
                        for q in range(KT_):
                            nc.tensor.transpose(ps[:, 2 + s, P * q:P * (q + 1)], prob[s][:, P * q:P * (q + 1)], ident[:])
                        nc.tensor.transpose(ps[0:NT, 4 + s, 256:256 + P], prob[s][:, PAST:NK], ident[:]).then_inc(prob_turned, 1)
                    else:
                        pe.wait_ge(prob_t_ready, cg + 3)
                        pe.wait_ge(o_taken, cg + 1)
                        pe.wait_ge(v_loaded[s], b * 32 + 32 * (m * NB + 1))
                        for p in range(n_pairs):
                            o = ps[:, 4 + s, M * p:M * (p + 1)]
                            for q in range(KT_):
                                nc.tensor.matmul(o, mix["vc"][:, s, q, P * p:P * (p + 1)],
                                                 prob_t[:, s, P * q + M * p:P * q + M * (p + 1)], start=q == 0, stop=False)
                            mm = nc.tensor.matmul(o, v_new[s][0:NT, P * p:P * (p + 1)],
                                                  prob_t[0:NT, s, PAST + M * p:PAST + M * (p + 1)], start=False, stop=True)
                        mm.then_inc(o_done, 1)
                pipelined(pe, (0, 1, 2, 3), stream)

            def project_out(base, m):
                first_pair(base, oh_ready, ol_ready, m * KD)
                pairs(base, 1, DOWN, KD, xh, xl)

            def indexer():
                for i in range(3 * IH):
                    q, h = i // IH + 1, i % IH
                    r = slice(DH * (h % 2), DH * (h % 2 + 1))
                    if i == 0:
                        pe.wait_ge(kt_copied, 2 * A_K + 1)
                        pe.wait_ge(nat_taken[0], A_K + A_V + 2)
                    if i >= 2:
                        pe.wait_ge(ix_relu, i - 1)
                    nc.tensor.matmul(ps[:, 4 + i % 2, 0:P * (q + 1)], qiT[r, h // 2, P * q:P * (q + 1)],
                                     kiT[r, 0:P * (q + 1)], start=True, stop=True).then_inc(ix_mm, 1)
                pe.wait_ge(nat_taken[1], A_K + A_V + 2)
                for b in range(NB + 1):
                    if b < NB:
                        pe.wait_ge(ki_loaded[b % 2], 16 * (b // 2 + 1))
                        if b >= 2:
                            pe.wait_ge(ki_ready, b - 1)
                        for q in range(KT_):
                            mm = nc.tensor.transpose(ps[0:DH, b % 2, P * q:P * (q + 1)], ki_c[:, b % 2, q, :], ident[:])
                        mm.then_inc(ki_turned, 1)
                    if b >= 1:
                        pe.wait_ge(ix_relu, 3 * IH + b)
                        pe.wait_ge(lw_ready, 1)
                        for lo, hi in ((0, PAST), (PAST, NK)):
                            mm = nc.tensor.matmul(flat[:, 3072 + lo:3072 + hi], lw[:, P * (b - 1):P * b],
                                                  score[(b - 1) % 2][:, lo:hi], start=b == 1, stop=b == NB)
                        mm.then_inc(ws_mm, 1)
                    if b < NB:
                        pe.wait_ge(ki_ready, b + 1)
                        pe.wait_ge(qib_ready, b + 1)
                        pe.wait_ge(ix_relu, 3 * IH + b)
                        nc.tensor.matmul(flat[:, 2048:2048 + PAST], qib[:, b % 2, :], ki_ct[:, b % 2, :], start=True, stop=True)
                        nc.tensor.matmul(flat[:, 2048 + PAST:2048 + NK], qib[:, b % 2, :],
                                         kiT[0:DH, SEQ + NT * b:SEQ + NT * (b + 1)], start=True, stop=True).then_inc(ix_mm, 1)

            def weights_by_row():
                nc.tensor.matmul(ps[:, 2, 0:P], rep[:], stage[1][0:IH, SEQ:T], start=True, stop=True).then_inc(lw_mm, 1)

            pe.wait_ge(s_in, 64)
            pe.wait_ge(s_const, 5)
            nc.tensor.transpose(ps[:, 4, 0:6 * KD], lnraw[:, 0, :], ident[0:6 * KD, 0:6 * KD])
            nc.tensor.transpose(ps[:, 4, 64:64 + 6 * KD], lnraw[:, 1, :], ident[0:6 * KD, 0:6 * KD]).then_inc(s_ln, 1)
            for k in range(KD):
                if k >= 2:
                    pe.wait_ge(x_ready, k - 1)
                for j in range(TT):
                    o = 1024 * (k % 2) + P * j
                    mm = nc.tensor.transpose(flat[:, o:o + P], xnat[:, j, P * k:P * (k + 1)], ident[:])
                mm.then_inc(x_turned, 1)
            pe.wait_ge(const_b, 19 + H)
            pe.wait_ge(slope_mm, 2)
            nc.tensor.matmul(ps[:, 5, 0:2], rep[:], nsl8[:], start=True, stop=True).then_inc(slope_mm, 1)
            pe.wait_ge(x_ready, KD)
            ffn(0, 0)
            statistics(0, a_in - 1)
            first_pair(a_in, xh_ready, xl_ready, KD)
            pairs(a_in, 1, A_Q, KD, xh, xl)
            with pe.Fori(0, A_K + A_V) as i:
                for s in range(2):
                    unit(s, i + (a_in + A_Q), KD, xh, xl)
                turn(i + (a_in + A_Q), i)
            attention(0)
            project_out(a_out, 0)
            statistics(1, a_out + DOWN - 1)
            ffn(1, 2 * KD)
            statistics(2, ffn_base[2] - 1)
            ffn(2, 3 * KD)
            statistics(3, b_in - 1)
            first_pair(b_in, xh_ready, xl_ready, 4 * KD)
            for i in (1, 2):
                for s in range(2):
                    unit(s, b_in + i, KD, xh, xl)
            turn(b_in + 2, A_K + A_V, (DH, IH), weights_by_row)
            indexer()
            pairs(b_in + 3, 0, 4, KD, xh, xl)
            for i in (7, 8):
                for s in range(2):
                    unit(s, b_in + i, KD, xh, xl)
                turn(b_in + i, A_K + A_V + i - 6, before=lambda: pe.wait_ge(cut_done, 5 + QT))
            attention(1)
            project_out(b_out, 1)
            statistics(4, b_out + DOWN - 1)
            ffn(3, 5 * KD)
            statistics(5, ffn_base[3] + FFN - 1)
            pe.wait_ge(x_ready, 7 * KD)
            for k in range(KD):
                if k >= 2:
                    pe.wait_ge(y_copied, k - 1)
                for j in range(TT):
                    o = 1024 * (k % 2) + P * j
                    mm = nc.tensor.transpose(flat[:, o:o + P], xres[:, k, P * j:P * (j + 1)], ident[:])
                mm.then_inc(y_turned, 1)


_OUTS = [("y_prompt", (1, 512, 1024)), ("y_sample", (8, 16, 1024)),
         ("a_k_prompt", (1, 1, 512, 16, 64)), ("a_v_prompt", (1, 1, 512, 16, 64)),
         ("a_k_sample", (1, 8, 16, 16, 64)), ("a_v_sample", (1, 8, 16, 16, 64)),
         ("b_k_prompt", (1, 1, 512, 4, 64)), ("b_v_prompt", (1, 1, 512, 4, 64)), ("b_idx_prompt", (1, 1, 512, 64)),
         ("b_k_sample", (1, 8, 16, 4, 64)), ("b_v_sample", (1, 8, 16, 4, 64)), ("b_idx_sample", (1, 8, 16, 64))]


def kernel(**inputs):
    import numpy as _np
    import concourse.bacc as _bacc
    from concourse import mybir as _mybir
    from concourse.bass_utils import run_bass_kernel_spmd as _run

    nc = _bacc.Bacc("TRN2", target_bir_lowering=False, num_devices=1)
    arrays, io = {}, {}
    for name, a in inputs.items():
        if name == "a_rel_bias":
            a = _np.asarray(a)[:, :, ::-1]
        a = _np.ascontiguousarray(a)
        arrays[f"in_{name}"] = a
        io[name] = nc.dram_tensor(f"in_{name}", a.shape, _mybir.dt.from_np(a.dtype), kind="ExternalInput").ap()
    for name, shape in _OUTS:
        io[name] = nc.dram_tensor(f"out_{name}", shape, _mybir.dt.float32, kind="ExternalOutput").ap()
    hybrid_encoder_step(nc, io)
    r = _run(nc, [arrays], core_ids=[0])
    return tuple(r.results[0][f"out_{name}"] for name, _ in _OUTS)
```

```python
from contextlib import ExitStack

import concourse.bass as bass
from concourse import mybir
from concourse.alu_op_type import AluOpType as ALU

ACT = mybir.ActivationFunctionType
F32 = mybir.dt.float32
F32R = mybir.dt.float32r
ds = bass.ds
P = 128
BIG = 1e30
TAKEN = -3e38


def row(t, i):
    if isinstance(i, int):
        return t[:, i, :]
    return t[:, ds(i, 1), :].rearrange("p a n -> p (a n)")


def hybrid_encoder_step(nc, io):
    SEQ, D = io["x_prompt"].shape[1:]
    NB, NT = io["x_sample"].shape[:2]
    F = io["ffn_w_gate"].shape[3]
    PAST = io["cache_a_k"].shape[2]
    H, DH = io["cache_a_k"].shape[3:]
    KV = io["cache_b_k"].shape[3]
    IH = io["b_w_in"].shape[2] - D - 2 * KV * DH
    IH = (IH - DH) // (DH + 1)
    CLIP = (io["a_rel_bias"].shape[2] - 1) // 2
    KD = D // P
    QT = SEQ // P
    TT = QT + NB * NT // P
    T = TT * P
    TH = T // 2
    FH = F // P // 2
    KMAX = max(FH, KD)
    NK = PAST + NT
    KT_ = PAST // P
    CH = 64
    LAG = 4
    ALPHA = 4.0 ** 0.25
    EPS = 1e-5
    SEL_P = min(256, SEQ // 4)
    SEL_S = min(256, NK // 4)
    L_EXT = NK + P

    UP, DOWN = FH, KD // 2
    FFN = 2 * (UP + DOWN)
    A_Q, A_K, A_V = 4, 4, 4
    A_IN, A_OUT, B_OUT = A_Q + A_K + A_V, 4, 4
    B_IN = 9
    ffn_base = [0, FFN + A_IN + A_OUT, 2 * FFN + A_IN + A_OUT, 3 * FFN + A_IN + A_OUT + B_IN + B_OUT]
    a_in, a_out = FFN, FFN + A_IN
    b_in = ffn_base[2] + FFN
    b_out = b_in + B_IN
    NORM_OF = [0, 2, 3, 5]
    UNITS_P = 4 * H
    UNITS_S = 2 * NB
    UNITS = UNITS_P + UNITS_S

    with ExitStack() as ctx:
        def sb(name, shape, dt=F32, c=ctx):
            return c.enter_context(nc.sbuf_tensor(name, shape, dt))

        def sem(name):
            return ctx.enter_context(nc.semaphore(name))

        def sems(name):
            return [sem(f"{name}{s}") for s in range(2)]

        xres = sb("xres", [P, KD, T])
        raw = [sb(f"raw{s}", [P, KMAX, P]) for s in range(2)]
        wh = [sb(f"wh{s}", [P, KMAX, P], F32R) for s in range(2)]
        wl = [sb(f"wl{s}", [P, KMAX, P], F32R) for s in range(2)]
        ident = sb("ident", [P, P])
        ones = sb("ones", [P, 1])
        one = sb("one", [P, P])
        eps = sb("eps", [P, 1])
        g_t = sb("g_t", [P, 6 * KD])
        b_t = sb("b_t", [P, 6 * KD])
        nat = sb("nat", [P, 2, T])
        big = sb("big", [P, 8, T])
        mx = sb("mx", [P, 2])
        rsum = sb("rsum", [P, 2])
        rinv = sb("rinv", [P, 2])
        zsum, qsum, sil, hf = (big[:, i, :] for i in (0, 1, 4, 5))
        diag = big[:, 2:4, :]
        sq = big[:, 6:8, :]
        stage = [sil, hf]
        score = [big[:, 0, :], big[:, 1, :]]
        prob = [big[:, 2, :], big[:, 3, :]]
        row4 = [*score, *prob]
        prob_t = sq
        v_new = [hf, sil]

        same_t = sb("same_t", [P, P])
        rep = sb("rep", [8, P])
        nslope = sb("nslope", [P, H])
        nslope_s = sb("nslope_s", [P, 2])
        nsl8 = sb("nsl8", [8, 2])
        frame = sb("frame", [P, 1])
        top8 = sb("top8", [P, 4, 8])
        mean, mean2, var, std, rstd = (sb(n, [P, TT]) for n in ("mean", "mean2", "var", "std", "rstd"))

        R0 = 88064

        def layout(name, first, second):
            with ExitStack() as c:
                got = [sb(n, s, d, c) for n, s, d in first]
                used = 0
                for n, s, d in first:
                    size = 4
                    for x in s[1:]:
                        size *= x
                    used += size
                assert used <= R0, (name, used)
                sb(f"{name}_pad", [P, (R0 - used) // 4], F32, c)
                return got + [sb(n, s, d, c) for n, s, d in second]

        hh, hl, xh, xl = layout("ffn", [("hh", [P, FH, T], F32R), ("hl", [P, FH, T], F32R)],
                                [("xh", [P, KD, T], F32R), ("xl", [P, KD, T], F32R)])
        xnat, lnraw = layout("pro", [("xnat", [P, TT, D], F32), ("lnraw", [6 * KD, 2, P], F32)], [])
        (a_qT, a_kT, a_v, a_kc_t, a_toep, a_bias_s, a_qb, a_kc, a_vc, a_qz) = layout(
            "a", [("a_qT", [P, KD, T], F32), ("a_kT", [P, KD, T], F32), ("a_v", [P, TT, D], F32),
                  ("a_kc_t", [P, 2, 4, NK], F32), ("a_toep", [P, 2, SEQ], F32),
                  ("a_bias_s", [P, 2, NK], F32), ("a_qb", [P, 2, P], F32)],
            [("a_kc", [P, 2, KT_, D // 2], F32), ("a_vc", [P, 2, KT_, D // 2], F32), ("a_qz", [P, 4, SEQ], F32)])
        a_onat = layout("ao", [("a_skip", [P, 2 * KD * T + TT * D], F32), ("a_onat", [P, QT, D], F32)], [])[1]
        (b_qT, b_kT, b_v, qiT, kiT, w_nat, dist, seen, b_mask_s, work, ki_c, ki_ct, lw, qib,
         b_kc_t, b_onat, b_qb, b_kc, b_vc, b_qz) = layout(
            "b", [("b_qT", [P, KD, T], F32), ("b_kT", [P, 2, T], F32), ("b_v", [P, TT, KV * DH], F32),
                  ("qiT", [P, 4, T], F32), ("kiT", [P, T], F32), ("w_nat", [P, TT, IH], F32),
                  ("dist", [P, SEQ], F32), ("seen", [P, 1280], F32), ("b_mask_s", [P, 2, NK], F32),
                  ("work", [P, 1152 + NK], F32), ("ki_c", [P, 2, KT_, DH], F32), ("ki_ct", [DH, 2, PAST], F32),
                  ("lw", [P, 9 * P], F32), ("qib", [DH, 2, P], F32)],
            [("b_kc_t", [P, 2, 1, NK], F32), ("b_onat", [P, QT, D], F32), ("b_qb", [P, 2, P], F32),
             ("b_kc", [P, 2, KT_, P], F32), ("b_vc", [P, 2, KT_, P], F32), ("b_qz", [P, 4, SEQ], F32)])
        ps = ctx.enter_context(nc.psum_tensor("ps", [P, 8, 512], F32))
        flat = ps[:, :, :].rearrange("p b n -> p (b n)")
        skewed = nc.dram_tensor("skewed", (H, P, L_EXT + P), F32, kind="Internal").ap()
        seen_tab = nc.dram_tensor("seen_tab", (P, NK), F32, kind="Internal").ap()

        raw_loaded = sems("raw_loaded")
        w_hi = sems("w_hi")
        w_lo = sems("w_lo")
        mm_done = sems("mm_done")
        out_taken = sems("out_taken")
        h_hi = sem("h_hi")
        h_lo = sem("h_lo")
        x_in = sems("x_in")
        ln_in = sem("ln_in")
        s_const = sem("s_const")
        zsum_done = sem("zsum_done")
        sq_done = sem("sq_done")
        qsum_done = sem("qsum_done")
        mean_done = sem("mean_done")
        msq_done = sem("msq_done")
        mean_copied = sem("mean_copied")
        m2_done = sem("m2_done")
        var_done = sem("var_done")
        std_done = sem("std_done")
        rstd_done = sem("rstd_done")
        diag_done = sem("diag_done")
        spread = sem("spread")
        centred = sem("centred")
        scaled = sem("scaled")
        x_ready = sem("x_ready")
        xh_ready = sem("xh_ready")
        xl_ready = sem("xl_ready")
        s_ln = sem("s_ln")
        y_turned = sem("y_turned")
        y_copied = sem("y_copied")
        x_turned = sem("x_turned")
        nat_stored = sems("nat_stored")
        v_stored = sem("v_stored")
        nat_turned = sems("nat_turned")
        nat_taken = sems("nat_taken")
        kt_copied = sem("kt_copied")
        s_done = sem("s_done")
        score_begun = sem("score_begun")
        score_done = sem("score_done")
        exp_done = sem("exp_done")
        rinv_done = sem("rinv_done")
        prob_turned = sem("prob_turned")
        prob_t_ready = sem("prob_t_ready")
        o_done = sem("o_done")
        o_taken = sem("o_taken")
        o_copied = sem("o_copied")
        o_turned = sem("o_turned")
        pnorm_done = sem("pnorm_done")
        qz_zero = sem("qz_zero")
        qz_ready = sem("qz_ready")
        toep_loaded = sems("toep_loaded")
        bias_ready = sem("bias_ready")
        onat_turned = sem("onat_turned")
        onat_taken = sems("onat_taken")
        k_loaded = sems("k_loaded")
        v_loaded = sems("v_loaded")
        kx_done = sems("kx_done")
        kx_taken = sems("kx_taken")
        qb_ready = sem("qb_ready")
        qb_zero = sem("qb_zero")
        oh_ready = sem("oh_ready")
        ol_ready = sem("ol_ready")
        tab_in = sem("tab_in")
        tab_built = sem("tab_built")
        tab_stored = sem("tab_stored")
        bias_s_loaded = sem("bias_s_loaded")
        ki_loaded = sems("ki_loaded")
        ix_mm = sem("ix_mm")
        ix_relu = sem("ix_relu")
        ix_acc = sem("ix_acc")
        is_mm = sem("is_mm")
        is_relu = sem("is_relu")
        ki_turned = sem("ki_turned")
        ki_ready = sem("ki_ready")
        qib_ready = sem("qib_ready")
        lw_ready = sem("lw_ready")
        lw_mm = sem("lw_mm")
        ws_mm = sem("ws_mm")
        top_done = sem("top_done")
        cut_done = sem("cut_done")
        seen_done = sem("seen_done")
        seen_stored = sem("seen_stored")
        mask_loaded = sems("mask_loaded")
        const_b = sem("const_b")
        dist_done = sem("dist_done")
        slope_mm = sem("slope_mm")

        def out2(s):
            return ps[:, 2 * s:2 * s + 2, 0:TH]

        dots_s = flat[:, 1024:1024 + NK]
        relu_s = prob
        spread_ps = [flat[:, 2048:2048 + T], flat[:, 3072:3072 + T]]

        def score_ps(c):
            return ps[:, (0, 1, 6, 7)[c % 4], :]

        def two(ap):
            return ap.rearrange("p (c n) -> p c n", c=2)

        def turned(s):
            return flat[:, 2048 + 1024 * s:2048 + 1024 * s + T].rearrange("p (j c) -> p j c", c=P)

        MIX = [dict(qT=a_qT, kT=a_kT, v=a_v, onat=a_onat, kc=a_kc, vc=a_vc, kc_t=a_kc_t, qb=a_qb, qz=a_qz,
                    pairs=4, kin=io["cache_a_k"], vin=io["cache_a_v"]),
               dict(qT=b_qT, kT=b_kT, v=b_v, onat=b_onat, kc=b_kc, vc=b_vc, kc_t=b_kc_t, qb=b_qb, qz=b_qz,
                    pairs=1, kin=io["cache_b_k"], vin=io["cache_b_v"])]

        def o_nat(m, s):
            return MIX[m]["qz"][:, 0, P * s:P * (s + 1)]

        def key_place(m, j):
            return (j // 2, j % 2) if m == 0 else (0, j // 4)

        def qz_slot(m, j):
            part = key_place(m, j)[1]
            return 2 * part + (j // 2 if m == 0 else j) % 2

        def kx_index(m, b, s, p):
            if m == 0:
                return b * 4 + (2 * s + p // 2)
            return b + 4 * NB

        def kx_bank(m, s, p):
            return p % 2 if m == 0 else s

        def pipelined(e, lags, body, peel=0):
            def step(t, s, b_of, live):
                for k, lag in enumerate(lags):
                    if live(lag):
                        body(b_of((s - lag) // 2), (s - lag) % 2, k)
            first = max((max(lags) + 1) // 2 * 2, peel)
            for t in range(first):
                step(t, t % 2, lambda d: t // 2 + d, lambda lag: t >= lag)
            with e.Fori(first // 2, NB) as b:
                for s in range(2):
                    step(None, s, lambda d: b + d, lambda lag: True)
            for t in range(2 * NB, 2 * NB + max(lags)):
                step(t, t % 2, lambda d: t // 2 + d, lambda lag: t - lag < 2 * NB)

        block = ctx.enter_context(nc.Block())

        @block.sync
        def _(sp):
            sp.dma_start(lnraw[:, 0, :], io["ln_g"].rearrange("l j (k p) -> (l j k) p", p=P)).then_inc(ln_in, 16)
            sp.dma_start(lnraw[:, 1, :], io["ln_b"].rearrange("l j (k p) -> (l j k) p", p=P)).then_inc(ln_in, 16)
            for half in range(2):
                c = slice(D // 2 * half, D // 2 * (half + 1))
                sp.dma_start(xnat[:, 0:TT - 1, c], io["x_prompt"].rearrange("o (j p) d -> p (o j) d", p=P)[:, :, c]).then_inc(x_in[half], 16)
                sp.dma_start(xnat[:, TT - 1, c], io["x_sample"].rearrange("b t d -> (b t) d")[:, c]).then_inc(x_in[half], 16)
                if half == 0:
                    sp.wait_ge(w_lo[0], 1)
                    wg, wu = (io[w][0, 0].rearrange("(k p) c -> p k c", p=P)[:, :, 0:P] for w in ("ffn_w_gate", "ffn_w_up"))
                    sp.dma_start(raw[0][:, 0:KD, :], wg).then_inc(raw_loaded[0], 16)
                    sp.wait_ge(w_lo[1], 1)
                    sp.dma_start(raw[1][:, 0:KD, :], wu).then_inc(raw_loaded[1], 16)
            sp.dma_start(nat[0:H, 0, 0:2 * CLIP + 1], io["a_rel_bias"][0]).then_inc(tab_in, 16)

            def load(s, n, src):
                sp.wait_ge(w_lo[s], n + 1)
                cols = src.shape[2]
                sp.dma_start(raw[s][:, 0:src.shape[1], 0:cols], src).then_inc(raw_loaded[s], 16)

            def load_tiles(w, n, i):
                for s in range(2):
                    load(s, n, w[:, :, ds(i * (2 * P) + s * P, P)])

            def ffn(f, skip):
                wg, wu, wd = (io[w][f // 2, f % 2].rearrange("(k p) c -> p k c", p=P)
                              for w in ("ffn_w_gate", "ffn_w_up", "ffn_w_down"))
                for half in range(2):
                    base = ffn_base[f] + half * (UP + DOWN)
                    with sp.Fori(skip if half == 0 else 0, UP) as i:
                        load(0, i + base, wg[:, :, ds((i + half * FH) * P, P)])
                        load(1, i + base, wu[:, :, ds((i + half * FH) * P, P)])
                    with sp.Fori(0, DOWN) as i:
                        for s in range(2):
                            load(s, i + (base + UP), wd[:, half * FH:(half + 1) * FH, ds(i * (2 * P) + s * P, P)])

            def store_tile(s, cols, dst_p, dst_s):
                view = nat[:, s, :].rearrange("p (j c) -> p j c", c=P)[:, :, 0:cols]
                sp.dma_start(dst_p, view[:, 0:QT, :]).then_inc(nat_stored[s], 16)
                sp.dma_start(dst_s, view[:, QT, :]).then_inc(nat_stored[s], 16)

            def rows_of(name, prompt):
                ap = io[name][0]
                if len(ap.shape) == 4:
                    ap = ap.rearrange("a b h d -> a b (h d)")
                return ap.rearrange("o (j p) c -> p (o j) c", p=P) if prompt else ap.rearrange("b t c -> (b t) c")

            def store_v(m):
                sp.wait_ge(nat_taken[0], 9 if m == 0 else 12)
                sp.wait_ge(nat_taken[1], 9 if m == 0 else 12)
                mix = MIX[m]
                sp.dma_start(rows_of("ab"[m] + "_v_prompt", True), mix["v"][:, 0:QT, :]).then_inc(v_stored, 16)
                sp.dma_start(rows_of("ab"[m] + "_v_sample", False), mix["v"][:, QT, :]).then_inc(v_stored, 16)

            def cached(m):
                mix = MIX[m]
                w = mix["pairs"] * P
                kin = mix["kin"][0].rearrange("b (j p) h d -> b p j (h d)", p=P)
                vin = mix["vin"][0].rearrange("b (j p) h d -> b p j (h d)", p=P)

                def unit(b, s, k):
                    waits = not isinstance(b, int) or b > 0
                    if k == 0:
                        if waits:
                            for bank in {kx_bank(m, s, p) for p in range(mix["pairs"])}:
                                p, ago = (2 + bank, 4) if m == 0 else (0, 1)
                                sp.wait_ge(kx_done[bank], kx_index(m, b, s, p) + (1 - ago))
                        kc = kin[ds(b, 1), :, :, s * w:(s + 1) * w].rearrange("o p j c -> p (o j) c")
                        sp.dma_start(mix["kc"][:, s, :, :], kc).then_inc(k_loaded[s], 16)
                        if m == 1:
                            if waits:
                                sp.wait_ge(bias_ready, b * 2 + (H + UNITS_P + s - 1))
                            sp.dma_start(b_mask_s[:, s, :], seen_rows(b)).then_inc(mask_loaded[s], 16)
                    else:
                        if waits:
                            sp.wait_ge(o_done, b * 2 + (m * UNITS + UNITS_P + s + 1))
                        vc = vin[ds(b, 1), :, :, s * w:(s + 1) * w].rearrange("o p j c -> p (o j) c")
                        sp.dma_start(mix["vc"][:, s, :, :], vc).then_inc(v_loaded[s], 16)
                        src = io["ab"[m] + "_v_sample"][0][ds(b, 1)].rearrange("o t h d -> (o t) (h d)")
                        sp.dma_start(v_new[s][0:NT, 0:w], src[:, s * w:(s + 1) * w]).then_inc(v_loaded[s], 16)

                def seen_rows(b):
                    return bass.AP(tensor=seen_tab.tensor, offset=b * (NT * NK), ap=[[0, 8], [NK, NT], [1, NK]])

                def first():
                    for k in range(2):
                        for s in range(2):
                            unit(0, s, k)

                def others():
                    pipelined(sp, (0, 3), lambda b, s, k: None if isinstance(b, int) and b == 0 else unit(b, s, k), peel=6)
                return first, others

            for w, s in ((io["ffn_w_gate"], 0), (io["ffn_w_up"], 1)):
                load(s, 1, w[0, 0].rearrange("(k p) c -> p k c", p=P)[:, :, P:2 * P])
            sp.wait_ge(tab_built, 2)
            tab = big[0:H, 6:8, :].rearrange("p a n -> p (a n)")[:, 0:L_EXT]
            sp.dma_start(bass.AP(tensor=skewed.tensor, offset=0, ap=[[P * (L_EXT + P), H], [L_EXT + P + 1, P], [1, L_EXT]]),
                         tab.unsqueeze(1).to_broadcast([H, P, L_EXT])).then_inc(tab_stored, 16)
            ffn(0, 2)
            wa = io["a_w_in"][0].rearrange("(k p) c -> p k c", p=P)
            with sp.Fori(0, A_Q + 2) as i:
                load_tiles(wa, i + a_in, i)
            sp.wait_ge(tab_stored, 16)
            for s in range(2):
                sp.wait_ge(mm_done[s], a_in + 1)
            for s in range(2):
                sp.dma_start(a_bias_s[:, s, :], skewed[8 * s:8 * s + 8, 0:NT, NK - PAST:2 * NK - PAST]).then_inc(bias_s_loaded, 16)

            def load_toep(h):
                sp.dma_start(a_toep[:, h % 2, :], skewed[h, :, NK - (SEQ - P):NK + P]).then_inc(toep_loaded[h % 2], 16)

            load_toep(0)
            load_toep(1)
            with sp.Fori(0, A_K) as i:
                load_tiles(wa, i + (a_in + A_Q + 2), i + (A_Q + 2))
                for s in range(2):
                    sp.wait_ge(nat_taken[s], i + 2)
                    c = ds(i * (2 * P) + s * P, P)
                    store_tile(s, P, rows_of("a_k_prompt", True)[:, :, c], rows_of("a_k_sample", False)[:, c])
            with sp.Fori(0, 2) as i:
                load_tiles(wa, i + (a_in + A_Q + A_K + 2), i + (A_Q + A_K + 2))
            wo = io["a_w_out"][0].rearrange("(k p) c -> p k c", p=P)
            with sp.Fori(0, 2) as i:
                load_tiles(wo, i + a_out, i)
            first, others = cached(0)
            for h in range(2, H):
                sp.wait_ge(score_done, 4 * (h - 1) + 2)
                load_toep(h)
                if h == 3:
                    store_v(0)
                if h == 5:
                    sp.wait_ge(v_stored, 32)
                    first()
            others()
            with sp.Fori(2, 4) as i:
                load_tiles(wo, i + a_out, i)
            ffn(1, 0)
            ffn(2, 0)
            wb = io["b_w_in"][0].rearrange("(k p) c -> p k c", p=P)
            q0, k0, v0, i0 = 0, D, D + KV * DH, D + 2 * KV * DH
            ki0 = i0 + IH * DH
            load_tiles(wb[:, :, i0:ki0], b_in, 0)
            load_tiles(wb[:, :, i0:ki0], b_in + 1, 1)
            load(0, b_in + 2, wb[:, :, ki0:ki0 + DH])
            load(1, b_in + 2, wb[:, :, ki0 + DH:ki0 + DH + IH])
            for s in range(2):
                sp.wait_ge(mm_done[s], b_in + 1)
            for b in range(NB):
                if b == 2:
                    load_tiles(wb, b_in + 3, 0)
                    load_tiles(wb, b_in + 4, 1)
                if b >= 2:
                    sp.wait_ge(ki_turned, b - 1)
                sp.dma_start(ki_c[:, b % 2, :, :], io["cache_b_idx"][0, b].rearrange("(j p) d -> p j d", p=P)).then_inc(ki_loaded[b % 2], 16)
            sp.wait_ge(nat_taken[0], 2 + A_K + A_V)
            store_tile(0, DH, rows_of("b_idx_prompt", True), rows_of("b_idx_sample", False))
            load_tiles(wb, b_in + 5, 2)
            load_tiles(wb, b_in + 6, 3)
            for s in range(2):
                load(s, b_in + 7, wb[:, :, k0 + s * P:k0 + (s + 1) * P])
            for s in range(2):
                load(s, b_in + 8, wb[:, :, v0 + s * P:v0 + (s + 1) * P])
            wo = io["b_w_out"][0].rearrange("(k p) c -> p k c", p=P)
            load_tiles(wo, b_out, 0)
            for s in range(2):
                sp.wait_ge(nat_taken[s], 3 + A_K + A_V)
                store_tile(s, P, rows_of("b_k_prompt", True)[:, :, s * P:(s + 1) * P],
                           rows_of("b_k_sample", False)[:, s * P:(s + 1) * P])
            load_tiles(wo, b_out + 1, 1)
            store_v(1)
            sp.wait_ge(seen_done, 9)
            sp.dma_start(seen_tab, work[:, 1152:1152 + NK]).then_inc(seen_stored, 16)
            sp.wait_ge(v_stored, 64)
            sp.wait_ge(seen_stored, 16)
            first, others = cached(1)
            first()
            others()
            with sp.Fori(2, 4) as i:
                load_tiles(wo, i + b_out, i)
            ffn(3, 0)
            for k in range(KD):
                sp.wait_ge(y_copied, k + 1)
                c = slice(P * k, P * (k + 1))
                store_tile(k % 2, P, io["y_prompt"][0, :, c].rearrange("(j p) c -> p j c", p=P),
                           io["y_sample"][:, :, c].rearrange("b t c -> (b t) c"))
            for s in range(2):
                sp.wait_ge(nat_stored[s], 32 * ([6, 5][s] + KD // 2))

        @block.gpsimd
        def _(pool):
            for s in range(2):
                pool.sem_inc(w_lo[s], 1)
            for s in (pnorm_done, pnorm_done):
                pool.sem_inc(s, 1)
            nc.gpsimd.memset(ident[:], 0.0).then_inc(s_const, 1)
            nc.gpsimd.memset(ones[:], 1.0 / D).then_inc(s_const, 1)
            nc.gpsimd.memset(eps[:], EPS).then_inc(s_const, 1)
            nc.gpsimd.memset(one[:], 1.0).then_inc(s_const, 1)
            pool.wait_ge(s_const, 4)
            nc.gpsimd.affine_select(out=ident[:], in_=ident[:], compare_op=ALU.not_equal, fill=1.0, base=0,
                                    pattern=[[-1, P]], channel_multiplier=1).then_inc(s_const, 1)

            def split_low(s, n, kt):
                pool.wait_ge(w_hi[s], n + 1)
                nc.gpsimd.tensor_tensor(wl[s][:, 0:kt, :], raw[s][:, 0:kt, :], wh[s][:, 0:kt, :].bitcast(F32),
                                        ALU.subtract).then_inc(w_lo[s], 1)

            def steps(base, count, kt, kt_next):
                if count > 1:
                    with pool.Fori(0, count - 1) as i:
                        for s in range(2):
                            split_low(s, i + (base + 1), kt)
                if kt_next:
                    for s in range(2):
                        split_low(s, base + count, kt_next)

            def x_low(base):
                for k in range(KD - 2):
                    pool.wait_ge(xh_ready, base + k + 1)
                    pool.wait_ge(x_ready, base + k + 1)
                    nc.gpsimd.tensor_tensor(xl[:, k, :], xres[:, k, :], xh[:, k, :].bitcast(F32),
                                            ALU.subtract).then_inc(xl_ready, 1)

            def ffn(f, kt_next):
                for half in range(2):
                    base = ffn_base[f] + half * (UP + DOWN)
                    steps(base, UP, KD, FH)
                    steps(base + UP, DOWN, FH, kt_next if half else KD)

            def constants_b():
                nc.gpsimd.memset(same_t[:], 0.0).then_inc(const_b, 1)
                for d in range(-7, 8):
                    pool.wait_ge(const_b, d + 8)
                    nc.gpsimd.affine_select(out=same_t[:], in_=same_t[:], compare_op=ALU.not_equal, fill=1.0,
                                            base=NT * d, pattern=[[-1, P]], channel_multiplier=1).then_inc(const_b, 1)
                nc.gpsimd.memset(rep[:], 1.0).then_inc(const_b, 1)
                pool.wait_ge(const_b, 17)
                nc.gpsimd.affine_select(out=rep[:], in_=rep[:], compare_op=ALU.is_ge, fill=0.0,
                                        base=0, pattern=[[1, P]], channel_multiplier=-NT).then_inc(const_b, 1)
                pool.wait_ge(const_b, 18)
                nc.gpsimd.affine_select(out=rep[:], in_=rep[:], compare_op=ALU.is_ge, fill=0.0,
                                        base=NT - 1, pattern=[[-1, P]], channel_multiplier=NT).then_inc(const_b, 1)
                for h in range(H):
                    nc.gpsimd.memset(nslope[:, h:h + 1], -(2.0 ** (-8.0 * (h + 1) / H))).then_inc(const_b, 1)

            def zero_buffers(m):
                mix = MIX[m]
                last = a_out if m == 0 else b_out
                for s in range(2):
                    pool.wait_ge(mm_done[s], last + 1)
                nc.gpsimd.memset(mix["qz"][:], 0.0).then_inc(qz_zero, 1)
                nc.gpsimd.memset(mix["qb"][:], 0.0).then_inc(qb_zero, 1)

            def cut_toep(h):
                pool.wait_ge(toep_loaded[h % 2], 16 * (h // 2 + 1))
                nc.gpsimd.memset(a_toep[0:CH, h % 2, SEQ - CH:SEQ], -BIG).then_inc(bias_ready, 1)

            def normalise(m):
                for u in range(UNITS_S):
                    cg = m * UNITS + UNITS_P + u
                    if m == 1:
                        mask_bias(u, cg)
                    pool.wait_ge(rinv_done, cg + 3)
                    pr = prob[u % 2][:, 0:NK]
                    nc.gpsimd.tensor_scalar(pr, pr, rinv[:, u % 2:u % 2 + 1], 1.0, ALU.mult, ALU.mult).then_inc(pnorm_done, 1)

            def mask_bias(u, cg):
                pool.wait_ge(mask_loaded[u % 2], 16 * (u // 2 + 1))
                pool.wait_ge(score_done, cg + 1)
                nc.gpsimd.tensor_scalar(nat[:, u % 2, 0:NK], b_mask_s[:, u % 2, :], nslope_s[:, u % 2:u % 2 + 1], 1.0,
                                        ALU.mult, ALU.mult).then_inc(bias_ready, 1)

            for s in range(2):
                split_low(s, 0, KD)
            constants_b()
            ffn(0, KD)
            x_low(KD)
            steps(a_in, A_IN, KD, None)
            zero_buffers(0)
            for h in range(2):
                cut_toep(h)
            for s in range(2):
                split_low(s, a_out, KD)
            for h in range(2, H):
                cut_toep(h)
            normalise(0)
            steps(a_out, A_OUT, KD, KD)
            x_low(2 * KD)
            ffn(1, KD)
            x_low(3 * KD)
            ffn(2, KD)
            x_low(4 * KD)
            pool.wait_ge(mm_done[0], b_in + 1)
            pool.wait_ge(mm_done[1], b_in + 1)
            nc.gpsimd.iota(dist[:], pattern=[[-1, SEQ]], base=SEQ - P, channel_multiplier=1,
                           allow_small_or_imprecise_dtypes=True).then_inc(dist_done, 1)
            nc.gpsimd.memset(lw[:], 0.0).then_inc(dist_done, 1)
            nc.gpsimd.iota(b_mask_s[:, 0, :], pattern=[[-1, NK]], base=PAST, channel_multiplier=0,
                           allow_small_or_imprecise_dtypes=True).then_inc(dist_done, 1)
            nc.gpsimd.iota(b_mask_s[:, 1, 0:NT], pattern=[[1, NT]], base=0, channel_multiplier=0,
                           allow_small_or_imprecise_dtypes=True).then_inc(dist_done, 1)
            steps(b_in, B_IN, KD, None)
            zero_buffers(1)
            pool.wait_ge(seen_done, 9)
            pool.wait_ge(nat_stored[0], 32 * 6)
            pool.wait_ge(nat_stored[1], 32 * 5)
            for h in range(H):
                for qt in range(QT):
                    c = UNITS + 4 * h + qt
                    pool.wait_ge(score_done, c + 1)
                    off = [0, 128, 384, 768][qt]
                    nc.gpsimd.tensor_scalar(nat[:, c % 2, 0:P * (qt + 1)], seen[:, off:off + P * (qt + 1)],
                                            nslope[:, h:h + 1], 1.0, ALU.mult, ALU.mult).then_inc(bias_ready, 1)
            normalise(1)
            steps(b_out, B_OUT, KD, KD)
            x_low(5 * KD)
            ffn(3, None)

        @block.scalar
        def _(act):
            def split_high(s, n, kt):
                act.wait_ge(raw_loaded[s], n * 16 + 16)
                act.wait_ge(mm_done[s], n + 1)
                nc.scalar.activation(wh[s][:, 0:kt, :], raw[s][:, 0:kt, :], ACT.Copy).then_inc(w_hi[s], 1)

            def up_step(n, i, kt_next, early=False):
                if early:
                    split_high(0, n + 1, kt_next)
                act.wait_ge(mm_done[0], n + 2)
                act.wait_ge(out_taken[1], n + 1)
                nc.scalar.activation(two(sil), out2(0), ACT.Silu).then_inc(out_taken[0], 1)
                if not early:
                    split_high(0, n + 1, kt_next)
                split_high(1, n + 1, kt_next)
                act.wait_ge(out_taken[1], n + 2)
                nc.scalar.activation(row(hh, i), hf, ACT.Copy).then_inc(h_hi, 1)

            def down_step(n, i, kt_next, norm, final=False):
                for s in range(2):
                    if kt_next and not (final and s):
                        split_high(s, n + 1, kt_next)
                    if norm is not None:
                        act.wait_ge(out_taken[s], n + 2)
                        act.wait_ge(qsum_done, i * 2 + (norm * (KD + 1) + 1))
                        nc.scalar.activation(sq[:, s, :], row(xres, i * 2 + s), ACT.Square).then_inc(sq_done, 1)
                if kt_next and final:
                    split_high(1, n + 1, kt_next)

            def down(base, norm, kt, kt_next):
                with act.Fori(0, DOWN - 1) as i:
                    down_step(i + base, i, kt, norm)
                down_step(base + DOWN - 1, DOWN - 1, kt_next, norm, final=True)

            def norm(L, last=False):
                act.wait_ge(var_done, L + 1)
                nc.scalar.activation(std[:], var[:], ACT.Sqrt, bias=eps[:, 0:1]).then_inc(std_done, 1)
                for k in range(KD):
                    act.wait_ge(scaled, L * KD + k + 1)
                    g, b = (t[:, L * KD + k:L * KD + k + 1] for t in (g_t, b_t))
                    if not last:
                        nc.scalar.activation(xh[:, k, :], sq[:, k % 2, :], ACT.Identity, scale=g, bias=b).then_inc(xh_ready, 1)
                    nc.scalar.activation(xres[:, k, :], sq[:, k % 2, :], ACT.Identity, scale=g, bias=b).then_inc(x_ready, 1)
                    if last and k >= 1:
                        y_out(k - 1)
                if last:
                    y_out(KD - 1)

            def y_out(k):
                act.wait_ge(y_turned, k + 1)
                act.wait_ge(nat_stored[k % 2], 32 * ([6, 5][k % 2] + k // 2))
                nc.scalar.activation(nat[:, k % 2, :], flat[:, 1024 * (k % 2):1024 * (k % 2) + T], ACT.Copy).then_inc(y_copied, 1)

            def ffn(f, kt_next):
                for half in range(2):
                    base = ffn_base[f] + half * (UP + DOWN)
                    up_step(base, 0, KD, early=half == 0)
                    with act.Fori(1, UP - 1) as i:
                        up_step(i + base, i, KD)
                    up_step(base + UP - 1, UP - 1, FH)
                    down(base + UP, NORM_OF[f] if half else None, FH, kt_next if half else KD)

            def project(n, dst, scale=1.0, early=False):
                for s in range(2):
                    if early:
                        split_high(s, n + 1, KD)
                    act.wait_ge(mm_done[s], n + 2)
                    nc.scalar.activation(two(dst(s)), out2(s), ACT.Copy, scale=scale).then_inc(out_taken[s], 1)
                    if not early:
                        split_high(s, n + 1, KD)

            def to_stage(n, t, scales=(1.0, 1.0)):
                for s in range(2):
                    act.wait_ge(mm_done[s], n + 2)
                    act.wait_ge(nat_taken[s], t + 1)
                    nc.scalar.activation(two(stage[s]), out2(s), ACT.Copy, scale=scales[s]).then_inc(out_taken[s], 1)
                    split_high(s, n + 1, KD)

            def exps(cg, s, w):
                act.wait_ge(score_done, cg + 3)
                act.wait_ge(prob_turned, cg + 1)
                act.wait_ge(rinv_done, cg + 1)
                nc.scalar.activation(prob[s][:, 0:w], score[s][:, 0:w], ACT.Exp, bias=mx[:, s:s + 1], scale=-1.0,
                                     accum_out=rsum[:, s:s + 1]).then_inc(exp_done, 1)

            def take_turned(cg, s, w):
                act.wait_ge(prob_turned, cg + 3)
                act.wait_ge(o_done, cg + 1)
                nc.scalar.activation(prob_t[:, s, 0:w], ps[:, 2 + s, 0:w], ACT.Copy).then_inc(prob_t_ready, 1)

            def attention(m):
                with act.Fori(0, 2) as g:
                    for c in range(32 + 2):
                        if c >= 2:
                            take_turned(g * 32 + (m * UNITS + c - 2), c % 2, P * ((c - 2) % QT + 1))
                        if c < 32:
                            cg, s, w = g * 32 + (m * UNITS + c), c % 2, P * (c % QT + 1)
                            act.wait_ge(score_done, cg + 3)
                            act.wait_ge(rinv_done, cg + 1)
                            nc.scalar.activation(row4[c % 4][:, 0:w], row4[c % 4][:, 0:w], ACT.Exp, bias=mx[:, s:s + 1],
                                                 scale=-1.0, accum_out=rsum[:, s:s + 1]).then_inc(exp_done, 1)
                for k in range(0, KD, 2):
                    act.wait_ge(onat_turned, m * KD + k + 1)
                    nc.scalar.activation(MIX[m]["qT"][:, k, 0:SEQ], ps[:, 6, :], ACT.Copy).then_inc(onat_taken[0], 1)
                mix = MIX[m]

                def stage(b, s, k):
                    cg = b * 2 + (m * UNITS + UNITS_P + s)
                    if k == 0:
                        for p in range(mix["pairs"]):
                            if kx_bank(m, s, p) == 0:
                                i = kx_index(m, b, s, p)
                                act.wait_ge(kx_done[0], i + 1)
                                act.wait_ge(s_done, cg - 1)
                                nc.scalar.activation(mix["kc_t"][:, s, p, 0:PAST], ps[:, 6, :], ACT.Copy).then_inc(kx_taken[0], 1)
                    elif k == 1:
                        if m == 1:
                            act.wait_ge(o_turned, b * 2 + (m * UNITS_S + s + 1))
                            v = ps[:, 4 + s, P:2 * P].rearrange("p (a e n) -> p a e n", e=2, n=NT)
                            for kv in range(2):
                                for e in range(2):
                                    q = nc.scalar.activation(
                                        mix["qT"][DH * e:DH * (e + 1), 4 * s + 2 * kv:4 * s + 2 * kv + 2, ds(b * NT + SEQ, NT)],
                                        v[DH * kv:DH * (kv + 1), 2 * kv:2 * kv + 2, e, :], ACT.Copy)
                            q.then_inc(o_taken, 1)
                    elif k == 2:
                        exps(cg, s, NK)
                    else:
                        act.wait_ge(prob_turned, cg + 3)
                        act.wait_ge(o_done, cg + 1)
                        nc.scalar.activation(prob_t[:, s, 0:PAST], ps[:, 2 + s, :], ACT.Copy)
                        nc.scalar.activation(prob_t[0:NT, s, PAST:PAST + P], ps[0:NT, 4 + s, 256:256 + P], ACT.Copy).then_inc(prob_t_ready, 1)
                pipelined(act, (0, 4, 1, 2), stage)

            for s in range(2):
                act.sem_inc(mm_done[s], 1)
                act.sem_inc(out_taken[s], 1)
                for t in (exp_done, prob_t_ready, prob_turned, o_done):
                    act.sem_inc(t, 1)
            for s in range(2):
                split_high(s, 0, KD)
            for k in range(KD):
                act.wait_ge(x_turned, k + 1)
                nc.scalar.activation(xres[:, k, :], flat[:, 1024 * (k % 2):1024 * (k % 2) + T], ACT.Copy).then_inc(x_ready, 1)
            ffn(0, KD)
            norm(0)
            project(a_in, lambda s: a_qT[:, s, :], DH ** -0.5, early=True)
            with act.Fori(1, A_Q) as i:
                project(i + a_in, lambda s: row(a_qT, i * 2 + s), DH ** -0.5)
            with act.Fori(0, A_K + A_V) as i:
                to_stage(i + (a_in + A_Q), i)
            attention(0)
            down(a_out, 1, KD, KD)
            norm(1)
            ffn(1, KD)
            norm(2)
            ffn(2, KD)
            norm(3)
            NAT_B = A_K + A_V
            for i in range(2):
                project(b_in + i, lambda s: qiT[:, 2 * i + s, :], DH ** -0.5, early=i == 0)
            to_stage(b_in + 2, NAT_B, (1.0, IH ** -0.5))
            for b in range(NB):
                for i in range(3 * IH // NB * b, 3 * IH // NB * (b + 1)):
                    act.wait_ge(ix_mm, i + 1)
                    if i >= 2:
                        act.wait_ge(ix_acc, i - 1)
                    w = P * (i // IH + 2)
                    nc.scalar.activation(score[i % 2][:, 0:w], ps[:, 4 + i % 2, 0:w], ACT.Relu).then_inc(ix_relu, 1)
                act.wait_ge(is_mm, b + 1)
                if b >= 2:
                    act.wait_ge(ws_mm, b - 1)
                nc.scalar.activation(relu_s[b % 2][:, 0:NK], dots_s, ACT.Relu).then_inc(is_relu, 1)
            with act.Fori(0, 4) as i:
                project(i + (b_in + 3), lambda s: row(b_qT, i * 2 + s), DH ** -0.5)
            to_stage(b_in + 7, NAT_B + 1)
            for s in range(2):
                act.wait_ge(out_taken[s], b_in + 9)
                nc.scalar.activation(b_kT[:, s, :], stage[s], ACT.Copy).then_inc(kt_copied, 1)
                act.wait_ge(nat_turned[s], NAT_B + 2)
                act.wait_ge(nat_stored[s], [32 * 5, 32 * 4][s])
                nc.scalar.activation(nat[:, s, :].rearrange("p (j c) -> p j c", c=P), turned(s), ACT.Copy).then_inc(nat_taken[s], 1)
            act.wait_ge(kt_copied, 2 * A_K + 3)
            to_stage(b_in + 8, NAT_B + 2)
            for s in range(2):
                act.wait_ge(nat_turned[s], NAT_B + 3)
                nc.scalar.activation(b_v[:, :, s * P:(s + 1) * P], turned(s), ACT.Copy).then_inc(nat_taken[s], 1)
            attention(1)
            down(b_out, 4, KD, KD)
            norm(4)
            ffn(3, None)
            norm(5, last=True)

        @block.vector
        def _(dve):
            def slopes():
                dve.wait_ge(const_b, 19 + H)
                for s in range(2):
                    if s:
                        dve.wait_ge(slope_mm, 1)
                    nc.vector.tensor_tensor_reduce(out=top8[0:8, s, :], in0=ident[0:8, 0:8], in1=nslope[0:8, 8 * s:8 * s + 8],
                                                   scale=1.0, scalar=0.0, op0=ALU.mult, op1=ALU.add,
                                                   accum_out=nsl8[:, s:s + 1]).then_inc(slope_mm, 1)
                dve.wait_ge(slope_mm, 3)
                nc.vector.tensor_copy(nslope_s[:], ps[:, 5, 0:2]).then_inc(s_const, 1)

            def up_step(n, i, hs):
                dve.wait_ge(mm_done[1], n + 2)
                dve.wait_ge(out_taken[0], n + 2)
                dve.wait_ge(h_lo, hs + 1)
                nc.vector.scalar_tensor_tensor(out=two(hf), in0=two(sil), scalar=0.5, in1=out2(1),
                                               op0=ALU.mult, op1=ALU.mult).then_inc(out_taken[1], 1)
                dve.wait_ge(h_hi, hs + 1)
                nc.vector.tensor_tensor(row(hl, i), hf, row(hh, i).bitcast(F32), ALU.subtract).then_inc(h_lo, 1)

            def down_step(n, i, first, norm, final=False):
                for s in range(2):
                    z = row(xres, i * 2 + s)
                    dve.wait_ge(mm_done[s], n + 2)
                    nc.vector.scalar_tensor_tensor(out=two(z), in0=two(z), scalar=ALPHA if first else 1.0,
                                                   in1=out2(s), op0=ALU.mult, op1=ALU.add).then_inc(out_taken[s], 1)
                    if norm is not None:
                        if not (final and s == 1):
                            dve.wait_ge(out_taken[s], n + 2)
                            dve.wait_ge(zsum_done, i * 2 + (norm * KD + s + 1))
                            nc.vector.tensor_tensor(zsum, zsum, z, ALU.add).then_inc(zsum_done, 1)
                        dve.wait_ge(sq_done, i * 2 + (norm * KD + s + 1))
                        dve.wait_ge(qsum_done, i * 2 + (norm * (KD + 1) + s + 1))
                        nc.vector.tensor_tensor(qsum, qsum, sq[:, s, :], ALU.add).then_inc(qsum_done, 1)

            def down(base, first, norm):
                if norm is not None:
                    nc.vector.memset(zsum, 0.0).then_inc(zsum_done, 1)
                    nc.vector.memset(qsum, 0.0).then_inc(qsum_done, 1)
                with dve.Fori(0, DOWN - 1) as i:
                    down_step(i + base, i, first, norm)
                down_step(base + DOWN - 1, DOWN - 1, first, norm, final=True)

            def on_diagonals(i, stat):
                nc.vector.tensor_tensor(diag[:, i, :].rearrange("p (j n) -> p j n", n=P),
                                        ident[:].unsqueeze(1).to_broadcast([P, TT, P]),
                                        stat[:].unsqueeze(2).to_broadcast([P, TT, P]), ALU.mult).then_inc(diag_done, 1)

            def norm(L, last=False):
                dve.wait_ge(mean_done, L + 1)
                nc.vector.tensor_copy(mean[:], ps[:, 6, 0:TT]).then_inc(mean_copied, 1)
                dve.wait_ge(mean_copied, L + 1)
                nc.vector.tensor_tensor(mean2[:], mean[:], mean[:], ALU.mult).then_inc(m2_done, 1)
                on_diagonals(0, mean)
                dve.wait_ge(m2_done, L + 1)
                dve.wait_ge(msq_done, L + 1)
                nc.vector.tensor_tensor(var[:], ps[:, 7, 0:TT], mean2[:], ALU.subtract).then_inc(var_done, 1)
                dve.wait_ge(std_done, L + 1)
                nc.vector.reciprocal(rstd[:], std[:]).then_inc(rstd_done, 1)
                dve.wait_ge(rstd_done, L + 1)
                on_diagonals(1, rstd)
                dve.wait_ge(spread, 2 * L + 1)
                for k in range(KD + 1):
                    if k < KD:
                        nc.vector.tensor_tensor(xres[:, k, :], xres[:, k, :], spread_ps[0], ALU.subtract).then_inc(centred, 1)
                    if k >= 1:
                        dve.wait_ge(centred, L * KD + k)
                        if k == 1:
                            dve.wait_ge(spread, 2 * L + 2)
                        if k >= 3:
                            dve.wait_ge(x_ready, (L + 1) * KD + k - 2)
                        nc.vector.tensor_tensor(sq[:, (k - 1) % 2, :], xres[:, k - 1, :], spread_ps[1],
                                                ALU.mult).then_inc(scaled, 1)
                if last:
                    return
                base = (L + 1) * KD
                dve.wait_ge(xl_ready, base + KD - 2)
                for k in range(KD - 2, KD):
                    dve.wait_ge(xh_ready, base + k + 1)
                    dve.wait_ge(x_ready, base + k + 1)
                    nc.vector.tensor_tensor(xl[:, k, :], xres[:, k, :], xh[:, k, :].bitcast(F32), ALU.subtract).then_inc(xl_ready, 1)

            def ffn(f):
                for half in range(2):
                    base = ffn_base[f] + half * (UP + DOWN)
                    with dve.Fori(0, UP) as i:
                        up_step(i + base, i, i + (2 * f + half) * UP)
                    if f == 0 and half:
                        dve.wait_ge(tab_stored, 16)
                    down(base + UP, half == 0, NORM_OF[f] if half else None)

            def keys(m, n, i, t, stores):
                for s in range(2):
                    dve.wait_ge(out_taken[s], n + 2)
                    nc.vector.tensor_copy(row(MIX[m]["kT"], i * 2 + s), stage[s]).then_inc(kt_copied, 1)
                    dve.wait_ge(nat_turned[s], t + 1)
                    if stores[s] is not None:
                        dve.wait_ge(nat_stored[s], stores[s])
                    nc.vector.tensor_copy(nat[:, s, :].rearrange("p (j c) -> p j c", c=P), turned(s)).then_inc(nat_taken[s], 1)

            def values(m, n, i, t):
                for s in range(2):
                    dve.wait_ge(nat_turned[s], t + 1)
                    nc.vector.tensor_copy(MIX[m]["v"][:, :, ds(i * (2 * P) + s * P, P)], turned(s)).then_inc(nat_taken[s], 1)

            def copy_q(m, g, j):
                mix = MIX[m]
                part = key_place(m, j)[1]
                src = row(mix["qT"], g * 4 + j // 2)[DH * (j % 2):DH * (j % 2 + 1), 0:SEQ]
                nc.vector.tensor_copy(mix["qz"][DH * part:DH * (part + 1), qz_slot(m, j), :], src).then_inc(qz_ready, 1)

            def bias_scores(cg, s, w, scores, bias, out=None):
                dve.wait_ge(s_done, cg + 1)
                dve.wait_ge(exp_done, cg + 1)
                dve.sem_inc(score_begun, 1)
                nc.vector.tensor_tensor_reduce(out=(score[s] if out is None else out)[:, 0:w], in0=scores, in1=bias,
                                               scale=-1.0, scalar=3e38, op0=ALU.add, op1=ALU.min, accum_out=mx[:, s:s + 1]).then_inc(score_done, 1)

            def invert_sum(cg, s):
                dve.wait_ge(exp_done, cg + 3)
                dve.wait_ge(o_taken, cg + 1)
                nc.vector.reciprocal(rinv[:, s:s + 1], rsum[:, s:s + 1]).then_inc(rinv_done, 1)

            def attention(m):
                mix = MIX[m]
                dve.wait_ge(qz_zero, m + 1)
                with dve.Fori(0, 2) as g:
                    for c in range(32 + 3):
                        if c < 32:
                            j, qt, w = c // 4, c % 4, P * (c % 4 + 1)
                            cg = g * 32 + (m * UNITS + c)
                            if c == 0:
                                copy_q(m, g, 0)
                            if qt == 0 and j + 1 < 8:
                                copy_q(m, g, j + 1)
                            if m == 0:
                                if qt == 0:
                                    dve.wait_ge(bias_ready, g * 8 + (j + 1))
                                bias = a_toep[:, j % 2, SEQ - w:SEQ]
                            else:
                                dve.wait_ge(bias_ready, g * 32 + (H + c + 1))
                                bias = nat[:, c % 2, 0:w]
                            dve.wait_ge(prob_turned, cg + (1 if c < 2 else -1))
                            bias_scores(cg, c % 2, w, score_ps(c)[:, 0:w], bias, row4[c % 4])
                        if c >= 3:
                            x = c - 3
                            dve.wait_ge(o_done, g * 32 + (m * UNITS + x + 3))
                            dve.wait_ge(rinv_done, g * 32 + (m * UNITS + x + 3))
                            nc.vector.tensor_scalar(mix["onat"][:, x % 4, ds(g * (8 * DH) + x // 4 * DH, DH)],
                                                    ps[:, 4 + x % 2, 0:DH], rinv[:, x % 2:x % 2 + 1], None,
                                                    ALU.mult).then_inc(o_taken, 1)
                        if 1 <= c < 33:
                            invert_sum(g * 32 + (m * UNITS + c - 1), (c - 1) % 2)
                for k in range(1, KD, 2):
                    dve.wait_ge(onat_turned, m * KD + k + 1)
                    nc.vector.tensor_copy(mix["qT"][:, k, 0:SEQ], ps[:, 7, :]).then_inc(onat_taken[1], 1)
                if m == 0:
                    dve.wait_ge(bias_s_loaded, 16 * 2)
                dve.wait_ge(qb_zero, m + 1)
                dve.wait_ge(o_taken, m * UNITS + UNITS_P + 2)

                def frames(b):
                    return ds(b * NT + SEQ, NT)

                def unit(b, s, k):
                    cg = b * 2 + (m * UNITS + UNITS_P + s)
                    qT, qb, t = mix["qT"], mix["qb"], frames(b)
                    if k == 0:
                        dve.wait_ge(s_done, cg - 1)
                        if m == 0:
                            v = qb[:, s, :].rearrange("p (a x) -> p a x", x=2 * NT)
                            nc.vector.tensor_copy(mix["kc_t"][:, s, :, PAST:NK], mix["kT"][:, 4 * s:4 * s + 4, t])
                            nc.vector.tensor_copy(v[0:DH, :, 0:NT], qT[0:DH, 4 * s:4 * s + 4, t])
                            nc.vector.tensor_copy(v[DH:P, :, NT:2 * NT], qT[DH:P, 4 * s:4 * s + 4, t]).then_inc(qb_ready, 1)
                        else:
                            v = qb[:, s, :].rearrange("p (a e n) -> p a e n", e=2, n=NT)
                            nc.vector.tensor_copy(mix["kc_t"][:, s, :, PAST:NK], mix["kT"][:, s:s + 1, t])
                            for kv in range(2):
                                for e in range(2):
                                    q = nc.vector.tensor_copy(v[DH * kv:DH * (kv + 1), 2 * kv:2 * kv + 2, e, :],
                                                              qT[DH * e:DH * (e + 1), 4 * s + 2 * kv:4 * s + 2 * kv + 2, t])
                            q.then_inc(qb_ready, 1)
                        for p in range(mix["pairs"]):
                            if kx_bank(m, s, p) == 1:
                                dve.wait_ge(kx_done[1], kx_index(m, b, s, p) + 1)
                                nc.vector.tensor_copy(mix["kc_t"][:, s, p, 0:PAST], ps[:, 7, :]).then_inc(kx_taken[1], 1)
                    elif k == 2:
                        if m == 1:
                            dve.wait_ge(bias_ready, b * 2 + (H + UNITS_P + s + 1))
                        bias_scores(cg, s, NK, flat[:, 0:NK], a_bias_s[:, s, :] if m == 0 else nat[:, s, 0:NK])
                        dve.wait_ge(pnorm_done, b * 2 + (m * UNITS_S + s + 1))
                        dve.wait_ge(exp_done, cg + 3)
                        nc.vector.reciprocal(rinv[:, s:s + 1], rsum[:, s:s + 1]).then_inc(rinv_done, 1)
                    elif k == 3:
                        dve.wait_ge(o_done, cg + 3)
                        if not isinstance(b, int) or b > 0:
                            dve.wait_ge(o_turned, b * 2 + (m * UNITS_S + s - 1))
                        nc.vector.tensor_copy(o_nat(m, s), ps[:, 4 + s, 0:P]).then_inc(o_copied, 1)
                    elif m == 0:
                        dve.wait_ge(o_turned, b * 2 + (m * UNITS_S + s + 1))
                        o = ps[:, 4 + s, P:2 * P]
                        v = o.rearrange("p (a x) -> p a x", x=2 * NT)
                        nc.vector.tensor_copy(qT[0:DH, 4 * s:4 * s + 4, t], v[0:DH, :, 0:NT])
                        q = nc.vector.tensor_copy(qT[DH:P, 4 * s:4 * s + 4, t], v[DH:P, :, NT:2 * NT])
                        q.then_inc(o_taken, 1)
                pipelined(dve, (0, 4, 1, 3), unit)
                dve.wait_ge(o_taken, (m + 1) * UNITS + 2)
                dve.wait_ge(onat_taken[0], (m + 1) * KD // 2)
                for k in range(KD):
                    nc.vector.tensor_copy(xh[:, k, :], mix["qT"][:, k, :]).then_inc(oh_ready, 1)
                    dve.wait_ge(oh_ready, m * KD + k + 1)
                    nc.vector.tensor_tensor(xl[:, k, :], mix["qT"][:, k, :], xh[:, k, :].bitcast(F32),
                                            ALU.subtract).then_inc(ol_ready, 1)

            def selection():
                dve.wait_ge(dist_done, 4)
                nc.vector.scalar_tensor_tensor(out=dist[:], in0=dist[:], scalar=-1.0, in1=dist[:], op0=ALU.mult,
                                               op1=ALU.max).then_inc(cut_done, 1)
                nc.vector.tensor_tensor_reduce(out=qib_scratch, in0=same_t[:, 0:NT], in1=b_mask_s[:, 1, 0:NT], scale=1.0,
                                               scalar=0.0, op0=ALU.mult, op1=ALU.add, accum_out=frame[:]).then_inc(cut_done, 1)
                dve.wait_ge(cut_done, 2)
                nc.vector.memset(dist[0:CH, SEQ - CH:SEQ], BIG).then_inc(cut_done, 1)
                nc.vector.tensor_scalar(b_mask_s[:, 0, :], b_mask_s[:, 0, :], frame[:, 0:1], None, ALU.add).then_inc(cut_done, 1)
                dve.wait_ge(cut_done, 4)
                nc.vector.scalar_tensor_tensor(out=b_mask_s[:, 0, :], in0=b_mask_s[:, 0, :], scalar=-1.0,
                                               in1=b_mask_s[:, 0, :], op0=ALU.mult, op1=ALU.max).then_inc(cut_done, 1)
                t = A_K + A_V
                dve.wait_ge(out_taken[0], b_in + 4)
                nc.vector.tensor_copy(kiT[0:DH, :], stage[0][0:DH, :])
                nc.vector.tensor_copy(kiT[DH:P, :], stage[0][0:DH, :]).then_inc(kt_copied, 1)
                dve.wait_ge(nat_turned[0], t + 1)
                dve.wait_ge(nat_stored[0], 32 * 4)
                nc.vector.tensor_copy(nat[:, 0, :].rearrange("p (j c) -> p j c", c=P)[:, :, 0:DH],
                                      turned(0)[:, :, 0:DH]).then_inc(nat_taken[0], 1)
                dve.wait_ge(nat_turned[1], t + 1)
                nc.vector.tensor_copy(w_nat[:], turned(1)[:, :, 0:IH]).then_inc(nat_taken[1], 1)
                dve.wait_ge(lw_mm, 1)
                nc.vector.tensor_tensor(lw[:].rearrange("p (b x) -> p b x", x=P + NT)[:, :, 0:NT],
                                        ps[:, 2, 0:P].rearrange("p (b x) -> p b x", x=NT),
                                        same_t[:].rearrange("p (b x) -> p b x", x=NT), ALU.mult).then_inc(lw_ready, 1)
                def stream(b):
                    v = qib[:, b % 2, :].rearrange("p (a e n) -> p a e n", e=2, n=NT)
                    f = slice(SEQ + NT * b, SEQ + NT * (b + 1))
                    if b >= 2:
                        dve.wait_ge(is_mm, b - 1)
                    nc.vector.tensor_copy(v[:, :, 0, :], qiT[0:DH, :, f])
                    nc.vector.tensor_copy(v[:, :, 1, :], qiT[DH:P, :, f]).then_inc(qib_ready, 1)
                    dve.wait_ge(ki_turned, b + 1)
                    nc.vector.tensor_copy(ki_ct[:, b % 2, :], ps[0:DH, b % 2, :]).then_inc(ki_ready, 1)

                dve.wait_ge(nat_taken[1], t + 2)
                for i in range(3 * IH):
                    q, h = i // IH + 1, i % IH
                    w, off = P * (q + 1), [0, 0, 256, 640][q]
                    if i % (3 * IH // NB) == 0:
                        stream(i // (3 * IH // NB))
                    dve.wait_ge(ix_relu, i + 1)
                    wk = work[:, off:off + w]
                    if h == 0:
                        nc.vector.tensor_scalar(wk, score[i % 2][:, 0:w], w_nat[:, q, 0:1], None, ALU.mult).then_inc(ix_acc, 1)
                    else:
                        dve.wait_ge(ix_acc, i)
                        nc.vector.scalar_tensor_tensor(out=wk, in0=score[i % 2][:, 0:w], scalar=w_nat[:, q, h:h + 1],
                                                       in1=wk, op0=ALU.mult, op1=ALU.add).then_inc(ix_acc, 1)
                dve.wait_ge(ix_acc, 3 * IH)
                tiles = []
                for q in range(1, QT):
                    w, off = P * (q + 1), [0, 0, 256, 640][q]
                    nc.vector.memset(work[0:CH, off + w - CH:off + w], TAKEN).then_inc(cut_done, 1)
                    tiles.append(work[:, off:off + w])
                dve.wait_ge(ws_mm, NB)
                tiles.append(work[:, 1152:1152 + NK])
                nc.vector.tensor_copy(tiles[3], flat[:, 3072:3072 + NK]).then_inc(cut_done, 1)
                n_cut, n_top = 5 + QT, 0
                rounds = [(SEL_P + 7) // 8] * 3 + [(SEL_S + 7) // 8]
                for r in range(max(rounds)):
                    live = [x for x in range(4) if r < rounds[x]]
                    first_cut, first_top = n_cut, n_top
                    for x in live:
                        dve.wait_ge(cut_done, max(first_cut - len(live), 0) + 1 + live.index(x) if r and len(live) == 4 else first_cut)
                        nc.vector.max(top8[:, x, :], tiles[x]).then_inc(top_done, 1)
                        n_top += 1
                    rest = SEL_S % 8 if r == rounds[3] - 1 else 0
                    if rest:
                        dve.wait_ge(top_done, n_top)
                        nc.vector.memset(top8[:, 3, rest:8], TAKEN).then_inc(top_done, 1)
                        n_top += 1
                    for y, x in enumerate(live):
                        dve.wait_ge(top_done, n_top if rest else first_top + y + 1)
                        nc.vector.match_replace(tiles[x], top8[:, x, :], tiles[x], TAKEN).then_inc(cut_done, 1)
                        n_cut += 1
                dve.wait_ge(cut_done, n_cut)
                nc.vector.tensor_copy(seen[:, 0:P], dist[:, SEQ - P:SEQ]).then_inc(seen_done, 1)
                outs = [seen[:, 128:384], seen[:, 384:768], seen[:, 768:1280], tiles[3]]
                for x in range(4):
                    nc.vector.tensor_scalar(outs[x], tiles[x], TAKEN / 2, BIG, ALU.is_gt, ALU.mult).then_inc(seen_done, 1)
                for x in range(4):
                    dve.wait_ge(seen_done, 2 + x)
                    d = b_mask_s[:, 0, :] if x == 3 else dist[:, SEQ - P * (x + 2):SEQ]
                    nc.vector.tensor_tensor(outs[x], outs[x], d, ALU.add).then_inc(seen_done, 1)

            qib_scratch = work[:, 0:NT]

            for s in range(2):
                for t in (score_done, rinv_done, o_taken):
                    dve.sem_inc(t, 1)
                dve.sem_inc(nat_taken[s], 1)
                dve.sem_inc(kx_taken[s], 1)
            dve.sem_inc(h_lo, 1)
            dve.wait_ge(tab_in, 16)
            tab = big[0:H, 6:8, :].rearrange("p a n -> p (a n)")
            rb = nat[0:H, 0, 0:2 * CLIP + 1]
            nc.vector.tensor_copy(tab[:, NK - CLIP:L_EXT], rb[:, 0:CLIP + P]).then_inc(tab_built, 1)
            nc.vector.tensor_copy(tab[:, 0:NK - CLIP], rb[:, 0:1].to_broadcast([H, NK - CLIP])).then_inc(tab_built, 1)
            dve.wait_ge(s_ln, 1)
            nc.vector.tensor_copy(g_t[:], ps[:, 4, 0:6 * KD]).then_inc(s_const, 1)
            nc.vector.tensor_copy(b_t[:], ps[:, 4, 64:64 + 6 * KD]).then_inc(s_const, 1)
            for k in range(KD):
                dve.wait_ge(x_ready, k + 1)
                nc.vector.tensor_copy(xh[:, k, :], xres[:, k, :]).then_inc(xh_ready, 1)
                dve.wait_ge(xh_ready, k + 1)
                nc.vector.tensor_tensor(xl[:, k, :], xres[:, k, :], xh[:, k, :].bitcast(F32), ALU.subtract).then_inc(xl_ready, 1)
            ffn(0)
            norm(0)
            slopes()
            keys(0, a_in + A_Q, 0, 0, [None, None])
            with dve.Fori(1, A_K) as i:
                keys(0, i + (a_in + A_Q), i, i, [i * 32, i * 32])
            with dve.Fori(0, A_V) as i:
                values(0, i + (a_in + A_Q + A_K), i, i + A_K)
            attention(0)
            down(a_out, True, 1)
            norm(1)
            ffn(1)
            norm(2)
            ffn(2)
            norm(3)
            selection()
            for s in range(2):
                dve.wait_ge(w_hi[s], b_out + 1)
                nc.vector.tensor_tensor(wl[s][:, 0:KD, :], raw[s][:, 0:KD, :], wh[s][:, 0:KD, :].bitcast(F32),
                                        ALU.subtract).then_inc(w_lo[s], 1)
            dve.wait_ge(kt_copied, 2 * A_K + 3)
            for s in range(2):
                dve.wait_ge(nat_taken[s], A_K + A_V + 4)
            attention(1)
            down(b_out, True, 4)
            norm(4)
            ffn(3)
            norm(5, last=True)

        @block.tensor
        def _(pe):
            def unit(s, n, kt, xa, xb, before=None):
                pe.wait_ge(w_lo[s], n + 2)
                pe.wait_ge(out_taken[s], n + 1)
                for k in range(kt):
                    if before:
                        before(k)
                    for j, (w, x) in enumerate(((wh[s], xa), (wh[s], xb), (wl[s], xa))):
                        for c in range(2):
                            mm = nc.tensor.matmul(ps[:, 2 * s + c, 0:TH], w[:, k, :], x[:, k, TH * c:TH * (c + 1)],
                                                  start=k == 0 and j == 0, stop=k == kt - 1 and j == 2)
                mm.then_inc(mm_done[s], 1)

            def first_pair(n, high, low, base):
                def products(s, parts, k, last=False):
                    for w, x in parts:
                        for c in range(2):
                            mm = nc.tensor.matmul(ps[:, 2 * s + c, 0:TH], w[:, k, :], x[:, k, TH * c:TH * (c + 1)],
                                                  start=k == 0 and w is wh[s] and x is xh, stop=last and x is xl)
                    if last:
                        mm.then_inc(mm_done[s], 1)

                for s in range(2):
                    pe.wait_ge(w_lo[s], n + 2)
                    pe.wait_ge(out_taken[s], n + 1)
                for t in range(KD + LAG):
                    if t < KD:
                        pe.wait_ge(high, base + t + 1)
                        products(0, [(wh[0], xh), (wl[0], xh)], t)
                    if 1 <= t <= KD:
                        pe.wait_ge(low, base + t)
                        products(0, [(wh[0], xl)], t - 1, t == KD)
                    if t >= LAG:
                        products(1, [(wh[1], xh), (wl[1], xh), (wh[1], xl)], t - LAG, t == KD + LAG - 1)

            def pairs(base, first, count, kt, xa, xb):
                if count > first:
                    with pe.Fori(first, count) as i:
                        for s in range(2):
                            unit(s, i + base, kt, xa, xb)

            def ffn(f, x_base):
                for half in range(2):
                    base = ffn_base[f] + half * (UP + DOWN)
                    hs = (2 * f + half) * UP
                    if half == 0:
                        first_pair(base, xh_ready, xl_ready, x_base)
                    pairs(base, 1 - half, UP, KD, xh, xl)

                    def wait_h(k):
                        if k in (0, FH - 1):
                            pe.wait_ge(h_lo, hs + (FH if k == 0 else FH + 1))
                    unit(0, base + UP, FH, hh, hl, wait_h)
                    unit(1, base + UP, FH, hh, hl)
                    pairs(base + UP, 1, DOWN, FH, hh, hl)

            def statistics(L, n):
                def sums(bank, of, first, last):
                    for j in range(TT):
                        mm = nc.tensor.matmul(ps[:, bank, j:j + 1], of[:, P * j:P * (j + 1)], ones[:, 0:1],
                                              start=first and j == 0, stop=last and j == TT - 1)
                    return mm
                pe.wait_ge(zsum_done, (L + 1) * KD)
                sums(6, zsum, True, False)
                pe.wait_ge(out_taken[1], n + 2)
                sums(6, xres[:, KD - 1, :], False, True).then_inc(mean_done, 1)
                pe.wait_ge(qsum_done, (L + 1) * (KD + 1))
                sums(7, qsum, True, True).then_inc(msq_done, 1)
                for i in range(2):
                    pe.wait_ge(diag_done, 2 * L + i + 1)
                    if i:
                        pe.wait_ge(var_done, L + 1)
                    for lo, hi in ((0, 512), (512, T)):
                        mm = nc.tensor.matmul(spread_ps[i][:, lo:hi], one[:], diag[:, i, lo:hi], start=True, stop=True)
                    mm.then_inc(spread, 1)

            def turn(n, t, rows=(P, P), before=None):
                for s in range(2):
                    pe.wait_ge(out_taken[s], n + 2)
                    pe.wait_ge(nat_taken[s], t + 1)
                    if before and s:
                        before()
                    r = rows[s]
                    for j in range(TT):
                        o = 2048 + 1024 * s + P * j
                        mm = nc.tensor.transpose(flat[:, o:o + r], stage[s][0:r, P * j:P * (j + 1)], ident[0:r, 0:r])
                    mm.then_inc(nat_turned[s], 1)

            def attention(m):
                mix = MIX[m]

                def scores(g, c):
                    j, qt, cg = c // 4, c % 4, g * 32 + (m * UNITS + c)
                    if qt == 0:
                        pe.wait_ge(qz_ready, g * 8 + (m * H + j + 1))
                    pe.wait_ge(score_done, cg + (1 if c == 0 else 0))
                    tile = g * 4 + j // 2 if m == 0 else g
                    nc.tensor.matmul(score_ps(c)[:, 0:P * (qt + 1)], mix["qz"][:, qz_slot(m, j), P * qt:P * (qt + 1)],
                                     row(mix["kT"], tile)[:, 0:P * (qt + 1)], start=True, stop=True).then_inc(s_done, 1)

                def turn_probs(g, c):
                    qt, cg = c % 4, g * 32 + (m * UNITS + c)
                    pe.wait_ge(exp_done, cg + 3)
                    pe.wait_ge(prob_t_ready, cg + 1)
                    for k in range(qt + 1):
                        mm = nc.tensor.transpose(ps[:, 2 + c % 2, P * k:P * (k + 1)], row4[c % 4][:, P * k:P * (k + 1)], ident[:])
                    mm.then_inc(prob_turned, 1)

                def outputs(g, c):
                    j, qt, cg = c // 4, c % 4, g * 32 + (m * UNITS + c)
                    pe.wait_ge(prob_t_ready, cg + 3)
                    pe.wait_ge(o_taken, cg + 1)
                    col = g * (8 * DH) + j * DH if m == 0 else g * (2 * DH) + j // 4 * DH
                    for k in range(qt + 1):
                        mm = nc.tensor.matmul(ps[:, 4 + c % 2, 0:DH], prob_t[:, c % 2, P * k:P * (k + 1)],
                                              mix["v"][:, k, ds(col, DH)], start=k == 0, stop=k == qt)
                    mm.then_inc(o_done, 1)

                with pe.Fori(0, 2) as g:
                    for c in range(32 + 3):
                        if c < 32:
                            scores(g, c)
                        if 2 <= c < 34:
                            turn_probs(g, c - 2)
                        if c >= 3:
                            outputs(g, c - 3)
                pe.wait_ge(o_taken, m * UNITS + UNITS_P + 2)
                for k in range(KD):
                    if k >= 2:
                        pe.wait_ge(onat_taken[k % 2], (m * KD + k) // 2)
                    for q in range(QT):
                        mm = nc.tensor.transpose(ps[:, 6 + k % 2, P * q:P * (q + 1)], mix["onat"][:, q, P * k:P * (k + 1)], ident[:])
                    mm.then_inc(onat_turned, 1)
                for s in range(2):
                    pe.wait_ge(onat_taken[s], (m + 1) * KD // 2)
                n_pairs = mix["pairs"]
                M = P // n_pairs

                def stream(b, s, k):
                    cg = b * 2 + (m * UNITS + UNITS_P + s)
                    if k == 0:
                        pe.wait_ge(k_loaded[s], b * 16 + 16 * (m * NB + 1))
                        for p in range(n_pairs):
                            bank = kx_bank(m, s, p)
                            pe.wait_ge(kx_taken[bank], kx_index(m, b, s, p) + 1)
                            for q in range(KT_):
                                mm = nc.tensor.transpose(ps[:, 6 + bank, P * q:P * (q + 1)],
                                                         mix["kc"][:, s, q, P * p:P * (p + 1)], ident[:])
                            mm.then_inc(kx_done[bank], 1)
                    elif k == 1:
                        pe.wait_ge(o_copied, b * 2 + (m * UNITS_S + s + 1))
                        nc.tensor.transpose(ps[:, 4 + s, P:2 * P], o_nat(m, s), ident[:]).then_inc(o_turned, 1)
                    elif k == 2:
                        for bank in {kx_bank(m, s, p) for p in range(n_pairs)}:
                            p = n_pairs - 2 + bank if m == 0 else 0
                            pe.wait_ge(kx_taken[bank], kx_index(m, b, s, p) + 2)
                        pe.wait_ge(qb_ready, b * 2 + (m * UNITS_S + s + 1))
                        pe.wait_ge(score_done, cg + 2)
                        for lo, hi in ((0, PAST), (PAST, NK)):
                            for p in range(n_pairs):
                                mm = nc.tensor.matmul(flat[M * p:M * (p + 1), lo:hi], mix["qb"][:, s, M * p:M * (p + 1)],
                                                      mix["kc_t"][:, s, p, lo:hi], start=True, stop=True)
                        mm.then_inc(s_done, 1)
                    elif k == 3:
                        pe.wait_ge(pnorm_done, b * 2 + (m * UNITS_S + s + 3))
                        pe.wait_ge(prob_t_ready, cg + 1)
                        pe.wait_ge(o_taken, cg + 1)
                        for q in range(KT_):
                            nc.tensor.transpose(ps[:, 2 + s, P * q:P * (q + 1)], prob[s][:, P * q:P * (q + 1)], ident[:])
                        nc.tensor.transpose(ps[0:NT, 4 + s, 256:256 + P], prob[s][:, PAST:NK], ident[:]).then_inc(prob_turned, 1)
                    else:
                        pe.wait_ge(prob_t_ready, cg + 3)
                        pe.wait_ge(o_taken, cg + 1)
                        pe.wait_ge(v_loaded[s], b * 32 + 32 * (m * NB + 1))
                        for q in range(KT_):
                            for p in range(n_pairs):
                                nc.tensor.matmul(ps[M * p:M * (p + 1), 4 + s, 0:P],
                                                 prob_t[:, s, P * q + M * p:P * q + M * (p + 1)],
                                                 mix["vc"][:, s, q, P * p:P * (p + 1)], start=q == 0, stop=False)
                        for p in range(n_pairs):
                            mm = nc.tensor.matmul(ps[M * p:M * (p + 1), 4 + s, 0:P],
                                                  prob_t[0:NT, s, PAST + M * p:PAST + M * (p + 1)],
                                                  v_new[s][0:NT, P * p:P * (p + 1)], start=False, stop=True)
                        mm.then_inc(o_done, 1)
                pipelined(pe, (0, 4, 1, 2, 3), stream)

            def project_out(base, m):
                first_pair(base, oh_ready, ol_ready, m * KD)
                pairs(base, 1, DOWN, KD, xh, xl)

            def indexer():
                def prompt(i):
                    q, h = i // IH + 1, i % IH
                    r = slice(DH * (h % 2), DH * (h % 2 + 1))
                    if i >= 2:
                        pe.wait_ge(ix_relu, i - 1)
                    nc.tensor.matmul(ps[:, 4 + i % 2, 0:P * (q + 1)], qiT[r, h // 2, P * q:P * (q + 1)],
                                     kiT[r, 0:P * (q + 1)], start=True, stop=True).then_inc(ix_mm, 1)

                def sum_heads(b):
                    pe.wait_ge(is_relu, b + 1)
                    for lo, hi in ((0, PAST), (PAST, NK)):
                        mm = nc.tensor.matmul(flat[:, 3072 + lo:3072 + hi], lw[:, P * b:P * (b + 1)],
                                              relu_s[b % 2][:, lo:hi], start=b == 0, stop=b == NB - 1)
                    mm.then_inc(ws_mm, 1)

                pe.wait_ge(kt_copied, 2 * A_K + 1)
                for s in range(2):
                    pe.wait_ge(nat_taken[s], A_K + A_V + 2)
                pe.wait_ge(lw_ready, 1)
                each = 3 * IH // NB
                for b in range(NB):
                    pe.wait_ge(ki_loaded[b % 2], 16 * (b // 2 + 1))
                    for q in range(KT_):
                        mm = nc.tensor.transpose(ps[0:DH, b % 2, P * q:P * (q + 1)], ki_c[:, b % 2, q, :], ident[:])
                    mm.then_inc(ki_turned, 1)
                    for i in range(each * b, each * (b + 1)):
                        prompt(i)
                    pe.wait_ge(ki_ready, b + 1)
                    pe.wait_ge(qib_ready, b + 1)
                    if b >= 1:
                        pe.wait_ge(is_relu, b)
                    nc.tensor.matmul(dots_s[:, 0:PAST], qib[:, b % 2, :], ki_ct[:, b % 2, :], start=True, stop=True)
                    nc.tensor.matmul(dots_s[:, PAST:NK], qib[:, b % 2, :],
                                     kiT[0:DH, SEQ + NT * b:SEQ + NT * (b + 1)], start=True, stop=True).then_inc(is_mm, 1)
                    if b >= 1:
                        sum_heads(b - 1)
                sum_heads(NB - 1)

            def weights_by_row():
                nc.tensor.matmul(ps[:, 2, 0:P], rep[:], stage[1][0:IH, SEQ:T], start=True, stop=True).then_inc(lw_mm, 1)

            pe.wait_ge(ln_in, 32)
            pe.wait_ge(s_const, 5)
            nc.tensor.transpose(ps[:, 4, 0:6 * KD], lnraw[:, 0, :], ident[0:6 * KD, 0:6 * KD])
            nc.tensor.transpose(ps[:, 4, 64:64 + 6 * KD], lnraw[:, 1, :], ident[0:6 * KD, 0:6 * KD]).then_inc(s_ln, 1)
            for k in range(KD):
                if k % (KD // 2) == 0:
                    pe.wait_ge(x_in[k // (KD // 2)], 32)
                if k >= 2:
                    pe.wait_ge(x_ready, k - 1)
                for j in range(TT):
                    o = 1024 * (k % 2) + P * j
                    mm = nc.tensor.transpose(flat[:, o:o + P], xnat[:, j, P * k:P * (k + 1)], ident[:])
                mm.then_inc(x_turned, 1)
            pe.wait_ge(x_ready, KD)
            ffn(0, 0)
            statistics(0, a_in - 1)
            first_pair(a_in, xh_ready, xl_ready, KD)
            pairs(a_in, 1, A_Q, KD, xh, xl)
            pe.wait_ge(slope_mm, 2)
            nc.tensor.matmul(ps[:, 5, 0:2], rep[:], nsl8[:], start=True, stop=True).then_inc(slope_mm, 1)
            pe.wait_ge(s_const, 8)
            with pe.Fori(0, A_K + A_V) as i:
                for s in range(2):
                    unit(s, i + (a_in + A_Q), KD, xh, xl)
                turn(i + (a_in + A_Q), i)
            attention(0)
            project_out(a_out, 0)
            statistics(1, a_out + DOWN - 1)
            ffn(1, 2 * KD)
            statistics(2, ffn_base[2] - 1)
            ffn(2, 3 * KD)
            statistics(3, b_in - 1)
            first_pair(b_in, xh_ready, xl_ready, 4 * KD)
            for i in (1, 2):
                for s in range(2):
                    unit(s, b_in + i, KD, xh, xl)
            turn(b_in + 2, A_K + A_V, (DH, IH), weights_by_row)
            indexer()
            pairs(b_in + 3, 0, 4, KD, xh, xl)
            for i in (7, 8):
                for s in range(2):
                    unit(s, b_in + i, KD, xh, xl)
                turn(b_in + i, A_K + A_V + i - 6, before=lambda: pe.wait_ge(cut_done, 5 + QT))
            attention(1)
            project_out(b_out, 1)
            statistics(4, b_out + DOWN - 1)
            ffn(3, 5 * KD)
            statistics(5, ffn_base[3] + FFN - 1)
            for k in range(KD):
                pe.wait_ge(x_ready, 6 * KD + k + 1)
                if k >= 2:
                    pe.wait_ge(y_copied, k - 1)
                for j in range(TT):
                    o = 1024 * (k % 2) + P * j
                    mm = nc.tensor.transpose(flat[:, o:o + P], xres[:, k, P * j:P * (j + 1)], ident[:])
                mm.then_inc(y_turned, 1)


_OUTS = [("y_prompt", (1, 512, 1024)), ("y_sample", (8, 16, 1024)),
         ("a_k_prompt", (1, 1, 512, 16, 64)), ("a_v_prompt", (1, 1, 512, 16, 64)),
         ("a_k_sample", (1, 8, 16, 16, 64)), ("a_v_sample", (1, 8, 16, 16, 64)),
         ("b_k_prompt", (1, 1, 512, 4, 64)), ("b_v_prompt", (1, 1, 512, 4, 64)), ("b_idx_prompt", (1, 1, 512, 64)),
         ("b_k_sample", (1, 8, 16, 4, 64)), ("b_v_sample", (1, 8, 16, 4, 64)), ("b_idx_sample", (1, 8, 16, 64))]


def kernel(**inputs):
    import numpy as _np
    import concourse.bacc as _bacc
    from concourse import mybir as _mybir
    from concourse.bass_utils import run_bass_kernel_spmd as _run

    nc = _bacc.Bacc("TRN2", target_bir_lowering=False, num_devices=1)
    arrays, io = {}, {}
    for name, a in inputs.items():
        if name == "a_rel_bias":
            a = _np.asarray(a)[:, :, ::-1]
        a = _np.ascontiguousarray(a)
        arrays[f"in_{name}"] = a
        io[name] = nc.dram_tensor(f"in_{name}", a.shape, _mybir.dt.from_np(a.dtype), kind="ExternalInput").ap()
    for name, shape in _OUTS:
        io[name] = nc.dram_tensor(f"out_{name}", shape, _mybir.dt.float32, kind="ExternalOutput").ap()
    hybrid_encoder_step(nc, io)
    r = _run(nc, [arrays], core_ids=[0])
    return tuple(r.results[0][f"out_{name}"] for name, _ in _OUTS)
```
